# Optimizing a Trainium2 kernel written in Bass

```python
import jax, jax.numpy as jnp
from jax import lax
import numpy as np

D_MODEL = 1024
BATCH = 1
SEQ = 2048
DEPTH = 1
DEC_BATCH = 1
DEC_SEQ = 32
PAST_LEN = 512

CHUNK = 64
WINDOW = 128
BAND_CHUNKS = WINDOW // CHUNK
CACHE_WIN = min(WINDOW, PAST_LEN)
HEAD_DIM = 64
N_Q_HEADS = 8
N_KV_HEADS = 2
GQA_GROUP = N_Q_HEADS // N_KV_HEADS
ATT_WIDTH = N_Q_HEADS * HEAD_DIM
KV_WIDTH = N_KV_HEADS * HEAD_DIM
ATT_SCALE = HEAD_DIM ** -0.5
RWKV_HEADS = 8
RWKV_HEAD = 64
RWKV_WIDTH = RWKV_HEADS * RWKV_HEAD
DECAY_LORA = 64
AAA_LORA = 64
GATE_LORA = 128
SHIFT_WIDTH = 3 * RWKV_WIDTH + DECAY_LORA + AAA_LORA + GATE_LORA
SHIFT_SPLITS = (RWKV_WIDTH, 2 * RWKV_WIDTH, 3 * RWKV_WIDTH,
                3 * RWKV_WIDTH + DECAY_LORA, 3 * RWKV_WIDTH + DECAY_LORA + AAA_LORA)
N_BRANCH = 2
GATE_WIDTH = N_BRANCH * D_MODEL
OFF_K = ATT_WIDTH
OFF_V = OFF_K + KV_WIDTH
OFF_RW = OFF_V + KV_WIDTH
OFF_GATE = OFF_RW + SHIFT_WIDTH
IN_WIDTH = OFF_GATE + GATE_WIDTH
D_FF = ((8 * D_MODEL + 3 * 256 - 1) // (3 * 256)) * 256
RMS_EPS = 1e-6
GN_EPS = 64e-5
NEG_INF = -1e30

kernel_name = 'hybrid_swa_sink_rwkv7_stream_step'

def rmsnorm(x, g):
    xf = x.astype(jnp.float32)
    y = xf * lax.rsqrt(jnp.mean(xf * xf, axis=-1, keepdims=True) + RMS_EPS)
    return (y * g.astype(jnp.float32)).astype(x.dtype)

def sink_softmax(s, sinks):
    sk = jnp.broadcast_to(sinks.astype(jnp.float32)[:, :, None, None], s.shape[:-1] + (1,))
    return jax.nn.softmax(jnp.concatenate([s, sk], axis=-1), axis=-1)[..., :-1]

def swa_prompt(q, k, v, sinks):
    B, T = q.shape[0], q.shape[1]
    nc = T // CHUNK
    qb = q.reshape(B, nc, CHUNK, N_KV_HEADS, GQA_GROUP, HEAD_DIM)
    kb = k.reshape(B, nc, CHUNK, N_KV_HEADS, HEAD_DIM)
    vb = v.reshape(B, nc, CHUNK, N_KV_HEADS, HEAD_DIM)
    pad = ((0, 0), (BAND_CHUNKS - 1, 0), (0, 0), (0, 0), (0, 0))
    kp, vp = jnp.pad(kb, pad), jnp.pad(vb, pad)
    kband = jnp.concatenate([kp[:, j:j + nc] for j in range(BAND_CHUNKS)], axis=2)
    vband = jnp.concatenate([vp[:, j:j + nc] for j in range(BAND_CHUNKS)], axis=2)
    key_chunk = (jnp.arange(nc)[:, None] - (BAND_CHUNKS - 1)
                 + jnp.arange(BAND_CHUNKS * CHUNK)[None, :] // CHUNK)
    valid = key_chunk >= 0
    s = jnp.einsum('bnqhgd,bnkhd->bnhgqk', qb, kband,
                   preferred_element_type=jnp.float32) * ATT_SCALE
    s = jnp.where(valid[None, :, None, None, None, :], s, NEG_INF)
    p = sink_softmax(s, sinks.reshape(N_KV_HEADS, GQA_GROUP))
    o = jnp.einsum('bnhgqk,bnkhd->bnqhgd', p.astype(v.dtype), vband)
    return o.reshape(B, T, ATT_WIDTH)

def swa_sample(q, k, v, cache_k, cache_v, sinks):
    B, S = q.shape[0], q.shape[1]
    keys = jnp.concatenate([cache_k, k.astype(cache_k.dtype)], axis=1)
    vals = jnp.concatenate([cache_v, v.astype(cache_v.dtype)], axis=1)
    q_chunk = (PAST_LEN + jnp.arange(S)) // CHUNK
    k_chunk = (PAST_LEN - CACHE_WIN + jnp.arange(CACHE_WIN + S)) // CHUNK
    valid = (k_chunk[None, :] <= q_chunk[:, None]) & (k_chunk[None, :] > q_chunk[:, None] - BAND_CHUNKS)
    qg = q.reshape(B, S, N_KV_HEADS, GQA_GROUP, HEAD_DIM)
    s = jnp.einsum('bqhgd,bkhd->bhgqk', qg, keys,
                   preferred_element_type=jnp.float32) * ATT_SCALE
    s = jnp.where(valid[None, None, None], s, NEG_INF)
    p = sink_softmax(s, sinks.reshape(N_KV_HEADS, GQA_GROUP))
    o = jnp.einsum('bhgqk,bkhd->bqhgd', p.astype(vals.dtype), vals)
    return o.reshape(B, S, ATT_WIDTH), keys[:, -CACHE_WIN:], vals[:, -CACHE_WIN:]

def rwkv7_mix(p, p_prev, S0, mu, w0, w2, a0, a2, g2, k_k, k_a, r_k, lnx_g, lnx_b):
    f32 = jnp.float32
    mu, w0, w2, a0, a2, g2, k_k, k_a, r_k, lnx_g, lnx_b = (
        t.astype(f32) for t in (mu, w0, w2, a0, a2, g2, k_k, k_a, r_k, lnx_g, lnx_b))
    B, T = p.shape[0], p.shape[1]
    pf = p.astype(f32)
    prev = jnp.concatenate([p_prev.astype(f32), pf[:, :-1]], axis=1)
    xs = pf + (prev - pf) * mu
    r, k, v, dw, da, dg = jnp.split(xs, SHIFT_SPLITS, axis=-1)
    w_log = -jax.nn.softplus(-(w0 + jnp.tanh(dw) @ w2)) - 0.5
    decay = jnp.exp(-jnp.exp(w_log))
    a = jax.nn.sigmoid(a0 + da @ a2)
    g = jax.nn.sigmoid(dg) @ g2
    hs = lambda t: t.reshape(B, T, RWKV_HEADS, RWKV_HEAD)
    kk = hs(k * k_k)
    kk = kk / jnp.maximum(jnp.sqrt(jnp.sum(kk * kk, axis=-1, keepdims=True)), 1e-12)
    k = k * (1.0 + (a - 1.0) * k_a)
    rh, kh, vh, wh, ah = hs(r), hs(k), hs(v), hs(decay), hs(a)

    def step(S, inp):
        r_t, w_t, k_t, v_t, kk_t, a_t = inp
        sa = jnp.einsum('bhij,bhj->bhi', S, -kk_t)
        S = (S * w_t[:, :, None, :] + sa[..., None] * (kk_t * a_t)[:, :, None, :]
             + v_t[..., None] * k_t[:, :, None, :])
        return S, jnp.einsum('bhij,bhj->bhi', S, r_t)

    tm = lambda t: jnp.moveaxis(t, 1, 0)
    S_T, o = lax.scan(step, S0.astype(f32), (tm(rh), tm(wh), tm(kh), tm(vh), tm(kk), tm(ah)))
    o = jnp.moveaxis(o, 0, 1)
    mean = jnp.mean(o, axis=-1, keepdims=True)
    var = jnp.mean(jnp.square(o - mean), axis=-1, keepdims=True)
    on = ((o - mean) * lax.rsqrt(var + GN_EPS)).reshape(B, T, RWKV_WIDTH) * lnx_g + lnx_b
    bonus = jnp.sum(rh * kh * r_k, axis=-1, keepdims=True) * vh
    out = (on + bonus.reshape(B, T, RWKV_WIDTH)) * g
    return out.astype(p.dtype), S_T, p[:, -1:]

def hybrid_layer(x, kv_cache, S0, shift0, norm1_g, w_in, attn_sinks, mu_shift, w0, w2, a0, a2,
                 g2, k_k, k_a, r_k, lnx_g, lnx_b, w_branch, w_out, norm2_g,
                 w_ffn_gate, w_ffn_up, w_ffn_down):
    B, T = x.shape[0], x.shape[1]
    h = rmsnorm(x, norm1_g)
    proj = h @ w_in
    q = proj[..., :OFF_K].reshape(B, T, N_Q_HEADS, HEAD_DIM)
    k = proj[..., OFF_K:OFF_V].reshape(B, T, N_KV_HEADS, HEAD_DIM)
    v = proj[..., OFF_V:OFF_RW].reshape(B, T, N_KV_HEADS, HEAD_DIM)
    p_rw = proj[..., OFF_RW:OFF_GATE]
    gates = proj[..., OFF_GATE:].reshape(B, T, N_BRANCH, D_MODEL)
    if kv_cache is None:
        att = swa_prompt(q, k, v, attn_sinks)
        new_k, new_v = k[:, -CACHE_WIN:], v[:, -CACHE_WIN:]
    else:
        att, new_k, new_v = swa_sample(q, k, v, kv_cache[0], kv_cache[1], attn_sinks)
    rw, S_new, shift_new = rwkv7_mix(p_rw, shift0, S0, mu_shift, w0, w2, a0, a2, g2,
                                     k_k, k_a, r_k, lnx_g, lnx_b)
    branches = jnp.stack([att, rw.astype(att.dtype)], axis=2)
    u = jnp.einsum('btnc,ncd->btnd', branches, w_branch)
    merged = jnp.sum(jax.nn.sigmoid(gates.astype(jnp.float32)) * u.astype(jnp.float32), axis=2)
    x = x + merged.astype(x.dtype) @ w_out
    h2 = rmsnorm(x, norm2_g)
    x = x + (jax.nn.silu(h2 @ w_ffn_gate) * (h2 @ w_ffn_up)) @ w_ffn_down
    return x, new_k, new_v, S_new.astype(x.dtype), shift_new

def setup_inputs(seed: int = 0) -> dict:
    key = jax.random.key(seed)
    ks = jax.random.split(key, 32)
    f32 = jnp.float32
    L = DEPTH
    nrm = lambda k, shape, scale: jax.random.normal(k, shape, f32) * scale
    return {
        'x_prompt': nrm(ks[0], (BATCH, SEQ, D_MODEL), 1.0),
        'x_sample': nrm(ks[1], (DEC_BATCH, DEC_SEQ, D_MODEL), 1.0),
        'cache_attn_k': nrm(ks[2], (L, DEC_BATCH, CACHE_WIN, N_KV_HEADS, HEAD_DIM), 1.0),
        'cache_attn_v': nrm(ks[3], (L, DEC_BATCH, CACHE_WIN, N_KV_HEADS, HEAD_DIM), 1.0),
        'state_rwkv': nrm(ks[4], (L, DEC_BATCH, RWKV_HEADS, RWKV_HEAD, RWKV_HEAD), 0.5),
        'state_shift': nrm(ks[5], (L, DEC_BATCH, 1, SHIFT_WIDTH), 1.0),
        'norm1_g': 1.0 + nrm(ks[6], (L, D_MODEL), 0.1),
        'w_in': nrm(ks[7], (L, D_MODEL, IN_WIDTH), D_MODEL ** -0.5),
        'attn_sinks': nrm(ks[8], (L, N_Q_HEADS), 1.0),
        'mu_shift': jax.random.uniform(ks[9], (L, SHIFT_WIDTH), f32),
        'w0': -1.0 + nrm(ks[10], (L, RWKV_WIDTH), 0.5),
        'w2': nrm(ks[11], (L, DECAY_LORA, RWKV_WIDTH), 0.5 * DECAY_LORA ** -0.5),
        'a0': nrm(ks[12], (L, RWKV_WIDTH), 0.1),
        'a2': nrm(ks[13], (L, AAA_LORA, RWKV_WIDTH), 0.5 * AAA_LORA ** -0.5),
        'g2': nrm(ks[14], (L, GATE_LORA, RWKV_WIDTH), GATE_LORA ** -0.5),
        'k_k': 1.0 + nrm(ks[15], (L, RWKV_WIDTH), 0.1),
        'k_a': 1.0 + nrm(ks[16], (L, RWKV_WIDTH), 0.1),
        'r_k': nrm(ks[17], (L, RWKV_HEADS, RWKV_HEAD), 0.1),
        'lnx_g': 1.0 + nrm(ks[18], (L, RWKV_WIDTH), 0.1),
        'lnx_b': nrm(ks[19], (L, RWKV_WIDTH), 0.02),
        'w_branch': nrm(ks[20], (L, N_BRANCH, ATT_WIDTH, D_MODEL), ATT_WIDTH ** -0.5),
        'w_out': nrm(ks[21], (L, D_MODEL, D_MODEL), D_MODEL ** -0.5),
        'norm2_g': 1.0 + nrm(ks[22], (L, D_MODEL), 0.1),
        'w_ffn_gate': nrm(ks[23], (L, D_MODEL, D_FF), D_MODEL ** -0.5),
        'w_ffn_up': nrm(ks[24], (L, D_MODEL, D_FF), D_MODEL ** -0.5),
        'w_ffn_down': nrm(ks[25], (L, D_FF, D_MODEL), D_FF ** -0.5),
        'final_norm_g': 1.0 + nrm(ks[26], (D_MODEL,), 0.1),
    }

def reference(x_prompt, x_sample, cache_attn_k, cache_attn_v, state_rwkv, state_shift,
              norm1_g, w_in, attn_sinks, mu_shift, w0, w2, a0, a2, g2, k_k, k_a, r_k,
              lnx_g, lnx_b, w_branch, w_out, norm2_g, w_ffn_gate, w_ffn_up, w_ffn_down,
              final_norm_g):
    xp, xs = x_prompt, x_sample
    Bp = xp.shape[0]
    S0_prompt = jnp.zeros((Bp, RWKV_HEADS, RWKV_HEAD, RWKV_HEAD), jnp.float32)
    shift0_prompt = jnp.zeros((Bp, 1, SHIFT_WIDTH), xp.dtype)
    kp_l, vp_l, sp_l, shp_l, ks_l, vs_l, ss_l, shs_l = [], [], [], [], [], [], [], []
    for l in range(DEPTH):
        lw = (norm1_g[l], w_in[l], attn_sinks[l], mu_shift[l], w0[l], w2[l], a0[l], a2[l],
              g2[l], k_k[l], k_a[l], r_k[l], lnx_g[l], lnx_b[l], w_branch[l], w_out[l],
              norm2_g[l], w_ffn_gate[l], w_ffn_up[l], w_ffn_down[l])
        xp, kp, vp, sp, shp = hybrid_layer(xp, None, S0_prompt, shift0_prompt, *lw)
        xs, kS, vS, sS, shS = hybrid_layer(xs, (cache_attn_k[l], cache_attn_v[l]),
                                           state_rwkv[l], state_shift[l], *lw)
        kp_l.append(kp); vp_l.append(vp); sp_l.append(sp); shp_l.append(shp)
        ks_l.append(kS); vs_l.append(vS); ss_l.append(sS); shs_l.append(shS)
    y_prompt = rmsnorm(xp, final_norm_g)
    y_sample = rmsnorm(xs, final_norm_g)
    return (y_prompt, y_sample,
            jnp.stack(kp_l), jnp.stack(vp_l), jnp.stack(sp_l), jnp.stack(shp_l),
            jnp.stack(ks_l), jnp.stack(vs_l), jnp.stack(ss_l), jnp.stack(shs_l))


_drawn_inputs = setup_inputs


def setup_inputs(seed=0):
    import zlib

    import numpy as np

    out = dict(_drawn_inputs(seed))
    spreads = {}
    factors = {'attn_sinks': 8.0, 'lnx_b': 8.0}
    for name, (base, spread) in spreads.items():
        noise = np.random.default_rng([zlib.crc32(name.encode()), seed]).standard_normal(out[name].shape)
        drawn = base * np.exp(spread * noise) if base else spread * noise
        out[name] = __import__('jax').numpy.asarray(drawn.astype(out[name].dtype))
    for name, factor in factors.items():
        out[name] = (out[name] * factor).astype(out[name].dtype)
    return out
```

```python
from contextlib import ExitStack

import concourse.bass as bass
from concourse import mybir

F32 = mybir.dt.float32
F32R = mybir.dt.float32r
ALU = mybir.AluOpType
ACT = mybir.ActivationFunctionType
AX = mybir.AxisListType.X

D = 1024
CH = 64
NSAMP = 32
KD = D // 128
DFF = 2816
NFF = DFF // 128
GROUPS = (8, 8, 6)
NRW = 14
NPL = 6 + NRW
BT = 512
NB = 4
MT = BT + CH
NPAIR = BT // 128
NTOK = CH + NB * BT
U_GA = NPL
U_BR = U_GA + KD
U_WO = U_BR + 2 * KD
U_F = [U_WO + KD + sum(2 * g + KD for g in GROUPS[:i]) for i in range(len(GROUPS))]
NU = U_F[-1] + 2 * GROUPS[-1] + KD
WU = KD * 128
SCALE = 64 ** -0.5
EXPM05 = 0.6065306597126334
LN2 = 0.6931471805599453
RMS_EPS = 1e-6
GN_EPS = 64e-5
C_MU, C_W0, C_A0, C_KK, C_KA, C_RK, C_LG, C_LB = 0, 14, 18, 22, 26, 30, 34, 38
C_N1, C_N2, C_NF, C_SINK, NCOL = 42, 50, 58, 66, 70
M_ID, M_ONE, M_HEAD, M_MEAN, M_LM, M_YD, M_XD, NMAT = 0, 1, 2, 3, 4, 5, 6, 7
NEG = -1e30


def steps(engine, sample):
    chs = (0,) if sample else (0, 1)

    def each(*names):
        return [f"{n}{c}" for c in chs for n in names]

    def by(*names):
        return [f"{n}{c}" for n in names for c in chs]

    soft = ("sm", "mx", "mx2", "sub", "sk", "sum", "den", "rec", "pn")
    if engine == "V":
        s = [f"{n}0" for n in soft]
        s += ["t1", "t2", "t3", "g1", "g2", "z1", "a1", "n1", "z3", "z4", "a3", "a4", "lw"]
        s += ["lwm"] * sample + ["scan", "kt1", "kt2"] + ["ktm"] * sample + ["bb"] + ["bbm"] * sample
        s += ["at", "rt", "pc", "bt", "ktl", "bo1", "bo2"]
        s += ([] if sample else [f"{n}1" for n in soft]) + ["bv"]
        s += each("lmE", "lmO", "ydE", "ydO") + each("xd", "svE", "svO")
        s += by("pt2", "pt3", "dt", "rr", "tt")
        s += each("x", "saE", "saO", "st1", "st2", "o") + ["oc", "on", "km"]
        return s
    if engine == "A":
        s = ["vt0", "ex0", "es0", "et", "eg", "ksq", "z2", "a2", "gcp", "ptr0", "at0", "n2", "n3", "pm", "p", "ip"]
        s += [] if sample else ["vt1", "ex1", "es1", "ptr1", "at1"]
        return s + by("tok", "xy2", "xy4", "x8", "d", "zl", "g", "h") + each("o1") + ["osq", "v1", "v2"]
    if engine == "G":
        s = ["qb", "kvb", "xs1", "xs2", "xs3", "kk", "cm", "kkn", "kt3"]
        return s + each("yoE", "yoO", "pt1") + ["lg", "lb", "ob", "gate"]
    s = ["s0", "vt0", "kn", "z", "a", "g", "ptr0", "pv0"] + ([] if sample else ["s1", "vt1", "ptr1", "pv1"]) + ["bo"]
    s += by("lm") + each("xv", "tok") + by("s1_", "s2_", "s3_", "s4_") + each("s5_", "lv") + by("s6_", "s7_", "s8_")
    return s + each("q0", "o1", "sa", "ds", "o2") + ["mean", "var"]


class Pair:

    def __init__(self, g, tok):
        self.sample = g is None
        self.tok, self.chs = tok, (0,) if self.sample else (0, 1)
        self.w = CH * len(self.chs)
        self.n = len(self.chs)
        self.names = {e: steps(e, self.sample) for e in "VAGT"}
        if self.sample:
            self.base = dict.fromkeys("VAGT", 0)
        else:
            self.base = {e: g * len(steps(e, False)) + len(steps(e, True)) for e in "VAGT"}

    def at(self, engine, name):
        return self.base[engine] + (self.names[engine].index(name) + 1)

    def all(self, engine):
        return self.base[engine] + len(self.names[engine])


class Order:

    def __init__(self, pair, engine):
        self.names, self.n = pair.names[engine], 0

    def __call__(self, name):
        assert self.names[self.n] == name, (self.names[self.n], name)
        self.n += 1

    def end(self):
        assert self.n == len(self.names), self.names[self.n]


def hybrid_layer(nc, x, w, col, mats, loras, kv_cache, st_in, shift_in,
                 y, st_s, st_p, shift_s, shift_p, kv_s, kv_p):
    with ExitStack() as ctx:
        def sem(name):
            return ctx.enter_context(nc.semaphore(name))

        cursor = [17 * 1024]

        def place(name, shape, dt=F32, at=None):
            size = 4
            for n in shape[1:]:
                size *= n
            if at is None:
                at = cursor[0]
                cursor[0] += (size + 31) // 32 * 32
            return nc.alloc_sbuf_tensor_at(name, shape, dt, offset=at), at

        def new(name, shape, dt=F32):
            return place(name, shape, dt)[0]

        PLANE = 4 * MT
        hh, hl = new("hh", [128, KD, MT], F32R), new("hl", [128, KD, MT], F32R)
        at_p = cursor[0]
        q = new("q", [128, 4, MT])
        kvp = new("kvp", [128, 2, CH + MT])
        rwp = new("rwp", [128, NRW, 1 + MT])
        assert cursor[0] - at_p >= 16 * PLANE
        mh, _ = place("mh", [128, KD, MT], F32R, at_p)
        ml, _ = place("ml", [128, KD, MT], F32R, at_p + KD * PLANE)
        nsum, nrs, nt0, nt1 = (place(n, [128, MT], F32, at_p + (16 + i) * PLANE)[0]
                               for i, n in enumerate(("nsum", "nrs", "nt0", "nt1")))
        nt = [nt0, nt1]
        assert cursor[0] - at_p >= 20 * PLANE
        ga, at_ga = place("ga", [128, KD, MT])
        xin, _ = place("xin", [128, KD, MT], F32, at_ga)
        raw = [new(f"raw{i}", [128, WU]) for i in range(2)]
        wh = [new(f"wh{i}", [128, WU], F32R) for i in range(2)]
        wl = [new(f"wl{i}", [128, WU], F32R) for i in range(2)]
        cst = new("cst", [128, NCOL])
        mat = new("mat", [128, NMAT, 128])
        lora = new("lora", [128, 2, 512])
        bias = new("bias", [128, 4])
        scratch = new("scratch", [128, 2])
        scanm = new("scanm", [128, 8, CH])
        kvs = new("kvs", [128, 2, 128])
        rws = new("rws", [128, NRW, 1])
        vmask = new("vmask", [128, CH])
        kmask = new("kmask", [128, 2, 128])
        st = new("st", [128, 4, CH])
        pcol = new("pcol", [128, 4, 2])
        at_s = cursor[0]
        xs = new("xs", [128, NRW, 128])
        kk, zz, aa, gg, cc, pp, ip, kt = (new(n, [128, 4, 128]) for n in "kk_ zz_ aa_ gg_ cc_ pp_ ip_ kt_".split())
        ra = new("ra", [128, 8, 2, CH])
        bkk = new("bkk", [128, 8, 3, CH])
        at_lm = cursor[0]
        lm = [new(f"lm{c}", [128, 2, 4, 128]) for c in range(2)]
        tk = [new(f"tk{c}", [128, 4, 2, CH]) for c in range(2)]
        at_end = cursor[0]
        sv = [new(f"sv{c}", [128, 4, 2, CH]) for c in range(2)]
        yd, yo, xd, pt, zl = ([new(f"{n}{c}", [128, 4, CH]) for c in range(2)] for n in ("yd", "yo", "xd", "pt", "zl"))
        xy, xy4 = ([new(f"{n}{c}", [128, 2, 4, CH]) for c in range(2)] for n in ("xy", "xyb"))
        at_a = [at_lm]

        def attn(name, shape):
            t, a = place(name, shape, F32, at_a[0])
            size = 4
            for n in shape[1:]:
                size *= n
            at_a[0] = a + size
            assert at_a[0] <= at_end
            return t

        qb = attn("qb", [128, 4, 128])
        kvb = attn("kvb", [128, 2, CH + 128])
        sm = attn("sm", [128, 4, 128])
        ptk = attn("ptk", [128, 4, 128])
        vtk = attn("vtk", [128, 128])
        mxs = attn("mxs", [128, 4, 4])
        at_d = [at_s]

        def dense(name, shape, dt=F32):
            t, a = place(name, shape, dt, at_d[0])
            size = 4
            for n in shape[1:]:
                size *= n
            at_d[0] = a + size
            return t

        ath, atl, rwh, rwl = (dense(n, [128, 4, MT], F32R) for n in ("ath", "atl", "rwh", "rwl"))
        fh, _ = place("fh", [128, KD, MT], F32R, at_s)
        fl, _ = place("fl", [128, KD, MT], F32R, at_s + KD * PLANE)
        xres = dense("xres", [128, KD, MT])
        sq = [dense(f"sq{i}", [128, MT]) for i in range(2)]
        acc, rs, e1, e2 = (dense(n, [128, MT]) for n in ("acc", "rs", "e1", "e2"))
        cursor[0] = max(cursor[0], at_d[0])
        assert cursor[0] <= nc.sbuf_usable_end, cursor[0]
        PS = ctx.enter_context(nc.psum_tensor("PS", [128, 8, 512], F32))

        shift_sv = sem("shift_sv")
        ini = sem("ini")
        xin_ld = sem("xin_ld")
        xres_ld = sem("xres_ld")
        w_ld = [sem(f"w_ld{i}") for i in range(2)]
        hi_done, lo_done = sem("hi_done"), sem("lo_done")
        mm_done = sem("mm_done")
        bank_free = sem("bank_free")
        ga_exp, ga_done = sem("ga_exp"), sem("ga_done")
        gb_exp = sem("gb_exp")
        v_own = sem("v_own")
        rw = {"V": sem("dve_steps"), "A": sem("act_steps"), "G": sem("pool_steps"), "T": sem("pe_steps")}
        b_hi, b_lo = sem("b_hi"), sem("b_lo")
        m_sum, m_hi, m_lo = sem("m_sum"), sem("m_hi"), sem("m_lo")
        n1_sq, n1_sum, n1_ms, n1_rs = sem("n1_sq"), sem("n1_sum"), sem("n1_ms"), sem("n1_rs")
        n1_t, n1_hi, n1_lo = sem("n1_t"), sem("n1_hi"), sem("n1_lo")
        n2_sq, n2_sum, n2_ms, n2_rs = sem("n2_sq"), sem("n2_sum"), sem("n2_ms"), sem("n2_rs")
        n2_t, n2_hi, n2_lo = sem("n2_t"), sem("n2_hi"), sem("n2_lo")
        y_done, y_st = sem("y_done"), sem("y_st")
        f_exp, f_own, f_hi, f_lo = sem("f_exp"), sem("f_own"), sem("f_hi"), sem("f_lo")
        saved, lead = sem("saved"), sem("lead")
        s_reset = sem("s_reset")
        s_shift, s_sstate, s_out = sem("s_shift"), sem("s_sstate"), sem("s_out")

        ld = sem("ld")
        passed = sem("passed")

        LDALL = 16 * 6
        block = ctx.enter_context(nc.Block())

        def half(b0):
            return (2, MT // 2) if b0 else (1, BT)

        def view(ap, b0):
            h, n = half(b0)
            return ap.rearrange("p (h n) -> p h n", h=h)

        def psv(bank, b0):
            h, n = half(b0)
            return PS[:, bank:bank + h, 0:n]

        def T_(b0):
            return MT if b0 else BT

        def cv(c, n, width):
            return cst[:, c:c + n].unsqueeze(2).to_broadcast([128, n, width])

        def mrep(m, n, p0=0, p1=128, c0=0, c1=128):
            return mat[p0:p1, m, c0:c1].unsqueeze(1).to_broadcast([p1 - p0, n, c1 - c0])

        def mmd(u):
            return u + 3

        def free(u):
            return u + 3

        def summed(m, j):
            return m * (KD + 1) + (j + 2)

        def settled(eng):
            eng.sem_inc(passed, 1)

        def blocks(eng, body):
            body(eng, 0, True)
            with eng.Fori(1, NB) as b:
                body(eng, b, False)

        def ring(b, off, i=0):
            return b * NU + i * 2 + off

        def landed(b, off, i=0):
            return (b * (NU // 2) + i + (off // 2 + 1)) * 16

        @block.sync
        def _(sp):
            sp.dma_start(xin[:], x[:, :, 0:MT]).then_inc(xin_ld, 16)
            sp.dma_start(cst[:], col).then_inc(ld, 16)
            sp.dma_start(mat[:], mats).then_inc(ld, 16)
            sp.dma_start(lora[:], loras).then_inc(ld, 16)
            sp.dma_start(kvp[:, :, 0:CH], kv_cache[:, :, CH:2 * CH]).then_inc(ld, 16)
            sp.dma_start(st[:], st_in).then_inc(ld, 16)
            sp.dma_start(rws[:], shift_in).then_inc(ld, 16)
            sp.dma_start(kv_s[:, :, 0:128 - NSAMP], kv_cache[:, :, NSAMP:128]).then_inc(s_out, 16)

            def load_units(b, off, n):
                with sp.Fori(0, n // 2) as i:
                    for p in range(2):
                        sp.wait_ge(lo_done, ring(b, off + p - 1, i))
                        settled(sp)
                        sp.dma_start(raw[p][:], w[i * 2 + (off + p)]).then_inc(w_ld[p], 16)

            def body(sp, b, b0):
                if b0:
                    for p in range(2):
                        sp.dma_start(raw[p][:], w[p]).then_inc(w_ld[p], 16)
                    load_units(b, 2, NPL)
                    sp.wait_ge(bank_free, free(NPL - 1))
                    sp.wait_ge(shift_sv, 2)
                    sp.dma_start(shift_s, rws[:]).then_inc(s_shift, 16)
                    sp.dma_start(kv_s[:, :, 128 - NSAMP:128], kvp[:, :, CH:CH + NSAMP]).then_inc(s_out, 16)
                    sp.wait_ge(rw["V"], Pair(None, 0).at("V", "st20"))
                    sp.dma_start(st_s, st[:]).then_inc(s_sstate, 16)
                    load_units(b, NPL + 2, U_BR - NPL)
                else:
                    load_units(b, 0, U_BR + 2)
                sp.wait_ge(b_lo, b * 8 + 8)
                settled(sp)
                T = T_(b0)
                src = x[:, :, 0:MT] if b0 else x[:, :, bass.ds(b * BT + CH, BT)]
                sp.dma_start(xres[:, :, 0:T], src).then_inc(xres_ld, 16)
                load_units(b, U_BR + 2, U_F[0] - U_BR)
                sp.wait_ge(m_lo, b * KD + (KD + 1))
                settled(sp)
                sp.dma_start(xin[:, :, 0:BT], x[:, :, bass.ds(b * BT + MT, BT)]).then_inc(xin_ld, 16)
                load_units(b, U_F[0] + 2, NU - U_F[0] - 2)

            blocks(sp, body)
            sp.wait_ge(lo_done, NB * NU - 1)
            sp.dma_start(raw[0][:], w[0]).then_inc(w_ld[0], 16)
            sp.wait_ge(rw["V"], Pair(NB * NPAIR - 1, 0).all("V"))
            sp.dma_start(st_p, st[:]).then_inc(s_out, 16)
            sp.wait_ge(saved, 2 * NB)
            sp.dma_start(shift_p, rws[:]).then_inc(s_out, 16)
            sp.dma_start(kv_p, kvs[:]).then_inc(s_out, 16)
            sp.wait_ge(s_out, 16 * 5)
            sp.wait_ge(s_shift, 16)
            sp.wait_ge(s_sstate, 16)
            sp.wait_ge(y_st, 16 * KD * NB)

        def half_rows(par):
            return slice(64 * par, 64 * par + 64)

        @block.tensor
        def _(pe):
            def unit(b, b0, off, i, mh_, ml_, bank, back, planes=range(KD), k0=0, planes_lo=None, wait_k=None):
                u, p = ring(b, off, i), off % 2
                pe.wait_ge(hi_done, u + 1)
                pe.wait_ge(lo_done, u + 1)
                pe.wait_ge(bank_free, u + (3 - back))
                h, n = half(b0)
                for k in planes:
                    if wait_k:
                        pe.wait_ge(*wait_k(k))
                    cols = slice(128 * k, 128 * k + 128)
                    for a, (wt, mv) in enumerate(((wh[p], mh_), (wh[p], ml_), (wl[p], mh_))):
                        for f in range(h):
                            mm = pe.matmul(PS[:, bank + f, 0:n], wt[:, cols], mv[:, k - k0, f * n:f * n + n],
                                           start=(k == k0 and a == 0), stop=(k == planes[-1] and a == 2))
                return mm

            def norm_sum(b0, s, bank):
                h, n = half(b0)
                for f in range(h):
                    mm = pe.matmul(PS[:, bank + f, 0:n], mat[:, M_ONE], s[:, f * n:f * n + n], start=True, stop=True)
                return mm

            def pair_steps(b, b0, pr, i):
                step = Order(pr, "T")
                V, A, G = rw["V"], rw["A"], rw["G"]
                done = rw["T"]
                W, n = pr.w, pr.n

                def flat(t):
                    return t[:].rearrange("p a w -> p (a w)")[:, 0:4 * W]

                xsf = xs[:].rearrange("p a w -> p (a w)")

                def xsl(plane, a=0, z=None):
                    return xsf[:, plane * W + a:plane * W + (W if z is None else z)]

                def filler(f):
                    unit(b, b0, U_GA + f, i, hh, hl, 0, 1).then_inc(mm_done, 1)

                def scores(c):
                    if c == 0:
                        pe.wait_ge(G, pr.at("G", "kvb"))
                        pe.wait_ge(bank_free, b * NU + free(NPL - 1))
                        if not pr.sample:
                            pe.wait_ge(V, pr.base["V"])
                            pe.wait_ge(A, pr.base["A"])
                    else:
                        pe.wait_ge(A, pr.at("A", "ptr0"))
                    settled(pe)
                    for j in range(4):
                        for kv in range(2):
                            r = half_rows(kv)
                            mm = pe.matmul(PS[r, 2, 128 * j:128 * j + 128], qb[r, j, CH * c:CH * c + CH],
                                           kvb[r, 0, CH * c:CH * c + 128], start=True, stop=True)
                    step(f"s{c}")
                    mm.then_inc(done, 1)
                    if c:
                        pe.wait_ge(A, pr.at("A", "at0"))
                        settled(pe)
                    step(f"vt{c}")
                    pe.transpose(PS[:, 3, 0:128], kvb[:, 1, CH * c:CH * c + 128], mat[:, M_ID]).then_inc(done, 1)

                def weigh(c):
                    pe.wait_ge(V, pr.at("V", f"pn{c}"))
                    settled(pe)
                    for j in range(4):
                        mm = pe.transpose(PS[:, 2, 128 * j:128 * j + 128], sm[:, j, :], mat[:, M_ID])
                    step(f"ptr{c}")
                    mm.then_inc(done, 1)
                    pe.wait_ge(A, pr.at("A", f"ptr{c}"))
                    settled(pe)
                    for kv in range(2):
                        r = half_rows(kv)
                        out = PS[r, 3, 0:256].rearrange("p (a w) -> p a w", a=4)
                        mm = pe.matmul(out, vtk[:, r], ptk[:, :, r], start=True, stop=True)
                    step(f"pv{c}")
                    mm.then_inc(done, 1)

                if not pr.sample:
                    filler(0)
                scores(0)
                pe.wait_ge(A, pr.at("A", "ksq"))
                settled(pe)
                step("kn")
                pe.matmul(PS[:, 7, 0:4 * W], mat[:, M_HEAD], flat(pp), start=True, stop=True).then_inc(done, 1)
                pe.wait_ge(V, pr.at("V", "g2"))
                settled(pe)
                for name, bank, r, m, plane in (("z", 4, slice(0, 64), 0, 12), ("a", 5, slice(64, 128), 0, 12),
                                                ("g", 6, slice(0, 128), 1, 13)):
                    for j in range(4):
                        mm = pe.matmul(PS[:, bank, W * j:W * j + W], lora[r, m, 128 * j:128 * j + 128],
                                       xsf[r, plane * W:plane * W + W], start=True, stop=True)
                    step(name)
                    mm.then_inc(done, 1)
                if not pr.sample:
                    filler(1)
                weigh(0)
                if not pr.sample:
                    scores(1)
                    weigh(1)
                pe.wait_ge(V, pr.at("V", "bo2"))
                settled(pe)
                step("bo")
                pe.matmul(PS[:, 4, 0:4 * W], mat[:, M_HEAD], flat(cc), start=True, stop=True).then_inc(done, 1)

                for c in pr.chs:
                    pe.wait_ge(G, pr.at("G", "kt3"))
                    pe.wait_ge(V, pr.at("V", "bv"))
                    if c == 1:
                        pe.wait_ge(A, pr.at("A", "gcp"))
                    settled(pe)
                    for j in range(4):
                        for par in range(2):
                            r, x_ = half_rows(par), j * n + c
                            l = bkk[r, x_, 1 - par:3 - par, :].rearrange("p a w -> p (a w)")
                            m = ra[r, x_, :, :].rearrange("p a w -> p (a w)")
                            mm = pe.matmul(PS[:, 4 + 2 * c + par, 128 * j:128 * j + 128], l, m, start=True, stop=True)
                    step(f"lm{c}")
                    mm.then_inc(done, 1)

                def tiles(bank, col, lhs, rhs, turn=False):
                    for j in range(4):
                        for par in range(2):
                            src = half_rows(1 - par if turn else par)
                            mm = pe.matmul(PS[half_rows(par), bank, col + CH * j:col + CH * j + CH],
                                           lhs(src, j, par), rhs(src, j, par), start=True, stop=True)
                    return mm

                def of(t):
                    return lambda r, j, par: t[r, j, :]

                def part(t, k):
                    return lambda r, j, par: t[r, k, j, :]

                for c in pr.chs:
                    b0_, b1_ = 4 + 2 * c, 5 + 2 * c
                    pe.wait_ge(V, pr.at("V", f"ydO{c}"))
                    settled(pe)
                    tiles(b0_, 0, lambda r, j, par: ra[r, j * n + c, 1, :], lambda r, j, par: bkk[r, j * n + c, 1, :])
                    for j in range(4):
                        for par in range(2):
                            mm = pe.matmul(PS[half_rows(1 - par), b0_, 256 + CH * j:256 + CH * j + CH],
                                           xsl(8 + j, CH * c, CH * c + CH), mat[:, M_ID, half_rows(par)],
                                           start=True, stop=True)
                    step(f"xv{c}")
                    mm.then_inc(done, 1)
                    for j in range(4):
                        for par in range(2):
                            l = bkk[:, j * n + c, 1 - par:3 - par, :].rearrange("p a w -> p (a w)")
                            at = (2 * j + par) * CH
                            mm = pe.matmul(PS[:, b1_, at:at + CH], l, mat[:, M_ID, half_rows(par)],
                                           start=True, stop=True)
                    step(f"tok{c}")
                    mm.then_inc(done, 1)

                for c in pr.chs:
                    pe.wait_ge(V, pr.at("V", f"xd{c}"))
                    pe.wait_ge(A, pr.at("A", f"tok{c}"))
                    settled(pe)
                    tiles(5 + 2 * c, 0, of(yd[c]), of(xd[c]))
                    step(f"s1_{c}")
                    tiles(5 + 2 * c, 256, of(xd[c]), of(yd[c])).then_inc(done, 1)
                for c in pr.chs:
                    pe.wait_ge(V, pr.at("V", f"svO{c}"))
                    pe.wait_ge(A, pr.at("A", f"xy2{c}"))
                    pe.wait_ge(G, pr.at("G", f"pt1{c}"))
                    settled(pe)
                    tiles(4 + 2 * c, 0, part(xy[c], 1), part(xy[c], 0))
                    tiles(4 + 2 * c, 256, part(xy[c], 0), part(xy[c], 1))
                    step(f"s2_{c}")
                    tiles(5 + 2 * c, 0, part(xy[c], 0), of(pt[c])).then_inc(done, 1)
                for c in pr.chs:
                    pe.wait_ge(V, pr.at("V", f"pt2{c}"))
                    pe.wait_ge(A, pr.at("A", f"xy4{c}"))
                    settled(pe)
                    tiles(4 + 2 * c, 0, part(xy4[c], 1), part(xy4[c], 0))
                    step(f"s3_{c}")
                    tiles(5 + 2 * c, 0, part(xy4[c], 0), of(pt[c])).then_inc(done, 1)
                for c in pr.chs:
                    pe.wait_ge(V, pr.at("V", f"pt3{c}"))
                    pe.wait_ge(A, pr.at("A", f"x8{c}"))
                    settled(pe)
                    step(f"s4_{c}")
                    tiles(4 + 2 * c, 0, of(xd[c]), of(pt[c])).then_inc(done, 1)
                for c in pr.chs:
                    pe.wait_ge(V, pr.at("V", f"dt{c}"))
                    settled(pe)
                    step(f"s5_{c}")
                    tiles(5 + 2 * c, 0, of(pt[c]), lambda r, j, par: mat[r, M_ID, r]).then_inc(done, 1)
                    step(f"lv{c}")
                    tiles(4 + 2 * c, 0, lambda r, j, par: lm[c][r, par, j, CH:128],
                          lambda r, j, par: sv[c][r, j, par, :], turn=True).then_inc(done, 1)
                for c in pr.chs:
                    pe.wait_ge(A, pr.at("A", f"d{c}"))
                    pe.wait_ge(G, pr.at("G", f"pt1{c}"))
                    settled(pe)
                    tiles(5 + 2 * c, 0, of(yd[c]), of(yo[c]))
                    step(f"s6_{c}")
                    tiles(5 + 2 * c, 256, of(yo[c]), of(yd[c])).then_inc(done, 1)
                for c in pr.chs:
                    pe.wait_ge(A, pr.at("A", f"g{c}"))
                    settled(pe)
                    tiles(4 + 2 * c, 0, part(xy[c], 0), part(xy[c], 1))
                    step(f"s7_{c}")
                    tiles(5 + 2 * c, 0, part(xy[c], 1), of(pt[c])).then_inc(done, 1)
                for c in pr.chs:
                    pe.wait_ge(V, pr.at("V", f"rr{c}"))
                    pe.wait_ge(A, pr.at("A", f"h{c}"))
                    settled(pe)
                    step(f"s8_{c}")
                    tiles(4 + 2 * c, 0, of(xd[c]), of(pt[c])).then_inc(done, 1)
                for c in pr.chs:
                    b0_, b1_ = 4 + 2 * c, 5 + 2 * c
                    if c:
                        pe.wait_ge(V, pr.at("V", "st20"))
                    elif not pr.sample:
                        pe.wait_ge(s_reset, 2)
                    pe.wait_ge(V, pr.at("V", f"tt{c}"))
                    settled(pe)
                    step(f"q0{c}")
                    tiles(b1_, 0, lambda r, j, par: ra[r, j * n + c, 1, :], of(st)).then_inc(done, 1)
                    step(f"o1{c}")
                    tiles(b0_, 0, of(st), lambda r, j, par: ra[r, j * n + c, 0, :]).then_inc(done, 1)
                    pe.wait_ge(V, pr.at("V", f"x{c}"))
                    settled(pe)
                    step(f"sa{c}")
                    tiles(b1_, 0, of(pt[c]), of(yo[c])).then_inc(done, 1)
                    pe.wait_ge(V, pr.at("V", f"saO{c}"))
                    settled(pe)
                    for j in range(4):
                        for par in range(2):
                            mm = pe.matmul(PS[half_rows(par), b1_, CH * j:CH * j + CH], tk[c][:, j, par, :],
                                           sv[c][:, j, par, :], start=True, stop=True)
                    step(f"ds{c}")
                    mm.then_inc(done, 1)
                    pe.wait_ge(A, pr.at("A", f"o1{c}"))
                    settled(pe)
                    for j in range(4):
                        for par in range(2):
                            mm = pe.matmul(PS[half_rows(par), b0_, CH * j:CH * j + CH], sv[c][:, j, par, :],
                                           lm[c][:, par, j, 0:CH], start=True, stop=True)
                    step(f"o2{c}")
                    mm.then_inc(done, 1)
                pe.wait_ge(V, pr.at("V", f"o{pr.chs[-1]}"))
                settled(pe)
                step("mean")
                pe.matmul(PS[:, 4, 0:4 * W], mat[:, M_MEAN], flat(ip), start=True, stop=True).then_inc(done, 1)
                pe.wait_ge(A, pr.at("A", "osq"))
                settled(pe)
                step("var")
                pe.matmul(PS[:, 5, 0:4 * W], mat[:, M_MEAN], flat(aa), start=True, stop=True).then_inc(done, 1)
                step.end()

            def body(pe, b, b0):
                with pe.Fori(0, NPL // 2) as i:
                    for p in range(2):
                        wk = (lambda k: (n1_lo, b * KD + (k + 1))) if p == 0 else None
                        unit(b, b0, p, i, hh, hl, 2 * p, 2, wait_k=wk).then_inc(mm_done, 1)
                if b0:
                    pair_steps(b, b0, Pair(None, 0), None)
                with pe.Fori(0, NPAIR) as i:
                    pair_steps(b, b0, Pair(b * NPAIR + i, i * 128 + (CH if b0 else 0)), i)
                for e in "AV":
                    pe.wait_ge(rw[e], Pair(b * NPAIR + (NPAIR - 1), 0).all(e))
                settled(pe)
                with pe.Fori(0, KD) as d:
                    unit(b, b0, U_BR, d, hh, hl, 2, 2).then_inc(mm_done, 1)
                    unit(b, b0, U_BR + 1, d, ath, atl, 4, 2, range(4),
                         wait_k=lambda k: (b_lo, b * 8 + (k + 1)))
                    unit(b, b0, U_BR + 1, d, rwh, rwl, 6, 2, range(4, 8), 4,
                         wait_k=lambda k: (b_lo, b * 8 + (k + 1))).then_inc(mm_done, 1)
                with pe.Fori(0, KD // 2) as i:
                    for p in range(2):
                        unit(b, b0, U_WO + p, i, mh, ml, 2 * p, 2,
                             wait_k=lambda k: (m_lo, b * KD + (k + 2))).then_inc(mm_done, 1)
                pe.wait_ge(n2_sum, summed(b * 2, KD))
                settled(pe)
                norm_sum(b0, acc, 4).then_inc(n2_ms, 1)
                for s, g in enumerate(GROUPS):
                    with pe.Fori(0, g) as i:
                        for p in range(2):
                            wk = (lambda k: (n2_lo, b * KD + (k + 1))) if p == 0 and s == 0 else None
                            unit(b, b0, U_F[s] + p, i, hh, hl, 2 * p, 2, wait_k=wk).then_inc(mm_done, 1)
                    pe.wait_ge(f_lo, b * NFF + (sum(GROUPS[:s + 1]) + 1))
                    settled(pe)
                    with pe.Fori(0, KD // 2) as i:
                        for p in range(2):
                            unit(b, b0, U_F[s] + 2 * g + p, i, fh, fl, 2 * p, 2, range(g)).then_inc(mm_done, 1)
                    if s == 1:
                        pe.wait_ge(n1_sum, b * (KD + 1) + 2 * (KD + 1))
                        settled(pe)
                        norm_sum(False, nsum, 4).then_inc(n1_ms, 1)
                pe.wait_ge(n2_sum, summed(b * 2 + 1, KD))
                settled(pe)
                norm_sum(b0, acc, 6).then_inc(n2_ms, 1)

            pe.wait_ge(ld, LDALL)
            pe.wait_ge(n1_sum, KD + 1)
            norm_sum(True, nsum, 4).then_inc(n1_ms, 1)
            pe.matmul(PS[:, 6, 0:2], mat[:, M_ONE], mat[:, M_ONE, 0:2], start=True, stop=True).then_inc(mm_done, 2)
            blocks(pe, body)

        @block.scalar
        def _(act):
            def split(b, off, i, first=False):
                u, p = ring(b, off, i), off % 2
                act.wait_ge(w_ld[p], landed(b, off, i))
                if not isinstance(u, int) or u >= 2:
                    act.wait_ge(mm_done, mmd(u - 2) if isinstance(u, int) else u + 1)
                act.activation(wh[p][:], raw[p][:], ACT.Copy).then_inc(hi_done, 1)

            def squares(T, src, out, sem_sq, sem_sum, count):
                if not isinstance(count, int) or count > 0:
                    act.wait_ge(sem_sum, count)
                settled(act)
                act.activation(out[:, 0:T], src, ACT.Square).then_inc(sem_sq, 1)

            def rstd(T, b0, bank, out, sem_ms, ms, sem_rs, rsn):
                act.wait_ge(sem_ms, ms)
                act.activation(view(out[:, 0:T], b0), psv(bank, b0), ACT.Ln, bias=bias[:, 0:1],
                               scale=1.0 / D).then_inc(sem_rs, 1)
                act.wait_ge(sem_rs, rsn + 1)
                act.activation(out[:, 0:T], out[:, 0:T], ACT.Exp, scale=-0.5).then_inc(sem_rs, 1)

            def pair_steps(b, b0, pr, i):
                step = Order(pr, "A")
                V, A, G, Tn = rw["V"], rw["A"], rw["G"], rw["T"]
                W, n = pr.w, pr.n

                def v4(t):
                    return t[:].rearrange("p a w -> p (a w)")[:, 0:4 * W]

                xsf = xs[:].rearrange("p a w -> p (a w)")

                def go(name, out, in_, func, **kw):
                    step(name)
                    act.activation(out, in_, func, **kw).then_inc(A, 1)

                def gates_exp(f):
                    act.wait_ge(mm_done, mmd(ring(b, U_GA + f, i)))
                    settled(act)
                    act.activation(view(ga[:, i * 2 + f, 0:T_(b0)], b0), psv(0, b0), ACT.Exp,
                                   scale=-1.0).then_inc(ga_exp, 1)

                def soft(c):
                    act.wait_ge(Tn, pr.at("T", f"vt{c}"))
                    go(f"vt{c}", vtk[:], PS[:, 3, 0:128], ACT.Copy)
                    act.wait_ge(V, pr.at("V", f"sub{c}"))
                    go(f"ex{c}", sm[:], sm[:], ACT.Exp)
                    act.wait_ge(V, pr.at("V", f"sk{c}"))
                    go(f"es{c}", mxs[:, 1, :], mxs[:, 1, :], ACT.Exp)

                def weigh(c):
                    act.wait_ge(Tn, pr.at("T", f"ptr{c}"))
                    go(f"ptr{c}", ptk[:].rearrange("p a w -> p (a w)"), PS[:, 2, :], ACT.Copy)
                    act.wait_ge(Tn, pr.at("T", f"pv{c}"))
                    settled(act)
                    go(f"at{c}", q[:, :, bass.ds(pr.tok + CH * c, CH)] if not pr.sample else q[:, :, 0:CH],
                       PS[:, 3, 0:256].rearrange("p (a w) -> p a w", a=4), ACT.Copy)

                soft(0)
                act.wait_ge(G, pr.at("G", "xs3"))
                go("et", xsf[0:64, 12 * W:13 * W], xsf[0:64, 12 * W:13 * W], ACT.Exp, scale=2.0)
                go("eg", xsf[:, 13 * W:14 * W], xsf[:, 13 * W:14 * W], ACT.Exp, scale=-1.0)
                act.wait_ge(G, pr.at("G", "kk"))
                go("ksq", v4(pp), v4(kk), ACT.Square)
                if not pr.sample:
                    split(b, U_GA + 1, i)
                act.wait_ge(V, pr.at("V", "z1"))
                go("z2", v4(zz), v4(zz), ACT.Exp, scale=-1.0)
                act.wait_ge(V, pr.at("V", "a1"))
                go("a2", v4(aa), v4(aa), ACT.Exp, scale=-1.0)
                act.wait_ge(Tn, pr.at("T", "g"))
                go("gcp", v4(gg), PS[:, 6, 0:4 * W], ACT.Copy)
                if not pr.sample:
                    gates_exp(0)
                weigh(0)
                act.wait_ge(V, pr.at("V", "n1"))
                go("n2", v4(pp), v4(pp), ACT.Ln, scale=2.0 ** 20)
                act.wait_ge(A, pr.at("A", "n2"))
                go("n3", v4(pp), v4(pp), ACT.Exp, scale=-0.5, bias=bias[:, 2:3])
                act.wait_ge(G, pr.at("G", "cm"))
                go("pm", v4(zz), v4(zz), ACT.Exp)
                act.wait_ge(G, pr.at("G", "kkn"))
                go("p", v4(pp), v4(cc), ACT.Exp)
                go("ip", v4(ip), v4(cc), ACT.Exp, scale=-1.0)
                if not pr.sample:
                    gates_exp(1)
                    split(b, U_GA + 2, i)
                    soft(1)
                    weigh(1)

                def flat2(t):
                    return t[:].rearrange("p k a w -> p (k a w)")

                def fl(t):
                    return t[:].rearrange("p a w -> p (a w)")

                def copies(name, st_, out, bank, width):
                    for c in pr.chs:
                        act.wait_ge(Tn, pr.at("T", f"{st_}{c}"))
                        go(f"{name}{c}", out(c), PS[:, bank + 2 * c, 0:width], ACT.Copy)

                copies("tok", "tok", lambda c: tk[c][:].rearrange("p a k w -> p (a k w)"), 5, 512)
                copies("xy2", "s1_", lambda c: flat2(xy[c]), 5, 512)
                copies("xy4", "s2_", lambda c: flat2(xy4[c]), 4, 512)
                copies("x8", "s3_", lambda c: fl(xd[c]), 4, 256)
                copies("d", "s5_", lambda c: fl(yd[c]), 5, 256)
                copies("zl", "lv", lambda c: fl(zl[c]), 4, 256)
                copies("g", "s6_", lambda c: flat2(xy[c]), 5, 512)
                copies("h", "s7_", lambda c: fl(xd[c]), 4, 256)
                for c in pr.chs:
                    act.wait_ge(Tn, pr.at("T", f"o1{c}"))
                    go(f"o1{c}", v4(ip).rearrange("p (a w) -> p a w", a=4)[:, :, CH * c:CH * c + CH],
                       PS[:, 4 + 2 * c, 0:256].rearrange("p (a w) -> p a w", a=4), ACT.Copy)
                act.wait_ge(V, pr.at("V", "oc"))
                go("osq", v4(aa), v4(ip), ACT.Square)
                act.wait_ge(Tn, pr.at("T", "var"))
                go("v1", v4(zz), PS[:, 5, 0:4 * W], ACT.Ln, bias=bias[:, 1:2])
                act.wait_ge(A, pr.at("A", "v1"))
                go("v2", v4(zz), v4(zz), ACT.Exp, scale=-0.5)
                step.end()

            def body(act, b, b0):
                T = T_(b0)
                with act.Fori(0, NPL // 2) as i:
                    split(b, 1, i)
                    split(b, 2, i)
                if b0:
                    pair_steps(b, b0, Pair(None, 0), None)
                with act.Fori(0, NPAIR) as i:
                    pair_steps(b, b0, Pair(b * NPAIR + i, i * 128 + (CH if b0 else 0)), i)
                last = Pair(b * NPAIR + (NPAIR - 1), 0)
                act.wait_ge(rw["G"], last.all("G"))
                act.wait_ge(rw["V"], last.all("V"))
                act.wait_ge(rw["T"], last.all("T"))
                for j in range(8):
                    dst, src = (ath, q) if j < 4 else (rwh, rwp)
                    act.wait_ge(rw["A"], last.all("A"))
                    act.activation(dst[:, j % 4, 0:T], src[:, j % 4, 0:T], ACT.Copy).then_inc(b_hi, 1)
                with act.Fori(0, KD) as d:
                    split(b, U_BR + 1, d)
                    act.wait_ge(mm_done, mmd(ring(b, U_BR, d)))
                    act.wait_ge(m_sum, b * KD + d + 1)
                    if b0:
                        act.wait_ge(b_lo, 8)
                    else:
                        act.wait_ge(b_lo, b * 8 + 8)
                    act.activation(view(e1[:, 0:T], b0), psv(2, b0), ACT.Exp, scale=-1.0).then_inc(gb_exp, 1)
                    split(b, U_BR + 2, d)
                    act.wait_ge(m_sum, b * KD + d + 2)
                    settled(act)
                    act.activation(mh[:, d, 0:T], acc[:, 0:T], ACT.Copy).then_inc(m_hi, 1)
                with act.Fori(0, KD // 2) as i:
                    for p in range(2):
                        split(b, U_WO + p + 1, i)
                        act.wait_ge(bank_free, free(ring(b, U_WO + p, i)))
                        squares(T, xres[:, i * 2 + p, 0:T], sq[p], n2_sq, n2_sum, summed(b * 2, i * 2 + (p - 1)))
                if not b0:
                    act.wait_ge(y_done, b * KD)
                rstd(T, b0, 4, rs, n2_ms, b * 2 + 1, n2_rs, b * 4)
                for d in range(KD):
                    act.wait_ge(n2_t, b * KD + (d + 1))
                    act.activation(hh[:, d, 0:T], sq[d % 2][:, 0:T], ACT.Copy).then_inc(n2_hi, 1)
                for s, g in enumerate(GROUPS):
                    before = sum(GROUPS[:s])
                    with act.Fori(0, g) as i:
                        split(b, U_F[s] + 1, i)
                        f = b * NFF + i + before
                        act.wait_ge(mm_done, mmd(ring(b, U_F[s], i)))
                        act.wait_ge(bank_free, free(ring(b, U_F[s] - 1, i)))
                        act.activation(view(e1[:, 0:T], b0), psv(0, b0), ACT.Exp, scale=-1.0).then_inc(f_exp, 1)
                        split(b, U_F[s] + 2, i)
                        act.wait_ge(bank_free, free(ring(b, U_F[s] + 1, i)))
                        settled(act)
                        act.activation(fh[:, i, 0:T], acc[:, 0:T], ACT.Copy).then_inc(f_hi, 1)
                    with act.Fori(0, KD // 2) as i:
                        for p in range(2):
                            off = U_F[s] + 2 * g + p
                            split(b, off + 1, i)
                            if s == 1:
                                act.wait_ge(xin_ld, b * 16 + 32)
                                squares(BT, xin[:, i * 2 + p, 0:BT], nt[p], n1_sq, n1_sum,
                                        b * (KD + 1) + i * 2 + (p + KD + 1))
                            if s == 2:
                                act.wait_ge(n1_t, b * KD + i * 2 + (p + KD + 1))
                                settled(act)
                                act.activation(hh[:, i * 2 + p, 0:BT], nt[p][:, 0:BT], ACT.Copy).then_inc(n1_hi, 1)
                                act.wait_ge(bank_free, free(ring(b, off, i)))
                                squares(T, xres[:, i * 2 + p, 0:T], sq[p], n2_sq, n2_sum,
                                        summed(b * 2 + 1, i * 2 + (p - 1)))
                    if s == 1:
                        rstd(BT, False, 4, nrs, n1_ms, b + 2, n1_rs, b * 2 + 2)
                rstd(T, b0, 6, rs, n2_ms, b * 2 + 2, n2_rs, b * 4 + 2)
                for d in range(KD):
                    act.wait_ge(y_done, b * KD + (d + 1))
                    settled(act)
                    dst = y[:, d, 0:MT] if b0 else y[:, d, bass.ds(b * BT + CH, BT)]
                    act.dma_start(dst, xres[:, d, 0:T]).then_inc(y_st, 16)

            act.preload_act_table_set("natural_log_exp_and_others")
            act.wait_ge(ld, LDALL)
            act.wait_ge(ini, 3)
            for d in range(KD):
                act.wait_ge(xin_ld, 16)
                squares(MT, xin[:, d, :], nt[d % 2], n1_sq, n1_sum, d)
            rstd(MT, True, 4, nrs, n1_ms, 1, n1_rs, 0)
            split(0, 0, 0)
            for d in range(KD):
                act.wait_ge(n1_t, d + 1)
                act.activation(hh[:, d, :], nt[d % 2][:], ACT.Copy).then_inc(n1_hi, 1)
            blocks(act, body)

        @block.gpsimd
        def _(pool):
            def pair_steps(b, b0, pr, i):
                step = Order(pr, "G")
                V, A, G, Tn = rw["V"], rw["A"], rw["G"], rw["T"]
                W, n = pr.w, pr.n

                def own(name):
                    pool.wait_ge(G, pr.at("G", name))
                    settled(pool)

                def v4(t):
                    return t[:].rearrange("p a w -> p (a w)")[:, 0:4 * W].rearrange("p (a w) -> p a w", a=4)

                xsv = xs[:].rearrange("p a w -> p (a w)")[:, 0:NRW * W].rearrange("p (a w) -> p a w", a=NRW)

                def tt_(name, out, a, bb_, op):
                    step(name)
                    pool.tensor_tensor(out, a, bb_, op).then_inc(G, 1)

                def cols(t, off, width):
                    return t[:, :, off:off + width] if pr.sample else t[:, :, bass.ds(pr.tok + off, width)]

                if not pr.sample:
                    for e in "VAGT":
                        pool.wait_ge(rw[e], pr.base[e])
                settled(pool)
                step("qb")
                pool.tensor_copy(qb[:, :, 0:W], cols(q, 0, W)).then_inc(G, 1)
                step("kvb")
                pool.tensor_copy(kvb[:, :, 0:CH + W], cols(kvp, 0, CH + W)).then_inc(G, 1)
                tt_("xs1", xsv, cols(rwp, 0, W), cols(rwp, 1, W), ALU.subtract)
                own("xs1")
                tt_("xs2", xsv, xsv, cv(C_MU, NRW, W), ALU.mult)
                own("xs2")
                tt_("xs3", xsv, xsv, cols(rwp, 1, W), ALU.add)
                own("xs3")
                tt_("kk", v4(kk), xsv[:, 4:8], cv(C_KK, 4, W), ALU.mult)
                pool.wait_ge(V, pr.at("V", "scan"))
                settled(pool)
                tt_("cm", v4(zz), v4(cc), v4(zz), ALU.subtract)
                pool.wait_ge(A, pr.at("A", "n3"))
                settled(pool)
                tt_("kkn", v4(kk), v4(kk), v4(pp), ALU.mult)
                pool.wait_ge(V, pr.at("V", "ktl"))
                settled(pool)
                step("kt3")
                pool.tensor_copy(bkk[:, 0:4 * n, 2, :], bkk[:, 0:4 * n, 0, :]).then_inc(G, 1)
                for c in pr.chs:
                    for par, name in enumerate(("E", "O")):
                        r = half_rows(par)
                        own(("kt3" if c == 0 else "pt10") if par == 0 else f"yoE{c}")
                        pool.wait_ge(V, pr.at("V", f"lm{name}{c}"))
                        settled(pool)
                        tt_(f"yo{name}{c}", yo[c][r], lm[c][r, par, :, CH:128], mrep(M_YD, 4, 64 * par, 64 * par + 64, 64, 128),
                            ALU.mult)
                    pool.wait_ge(V, pr.at("V", f"ydO{c}"))
                    own(f"yoO{c}")
                    tt_(f"pt1{c}", pt[c][:], yd[c][:], mrep(M_XD, 4, c0=64, c1=128), ALU.add)
                pool.wait_ge(V, pr.at("V", "on"))
                settled(pool)
                tt_("lg", v4(ip), v4(ip), cv(C_LG, 4, W), ALU.mult)
                own("lg")
                tt_("lb", v4(ip), v4(ip), cv(C_LB, 4, W), ALU.add)
                own("lb")
                tt_("ob", v4(ip), v4(ip), v4(kt), ALU.add)
                own("ob")
                tt_("gate", cols(rwp[:, 0:4], 0, W), v4(ip), v4(gg), ALU.mult)
                step.end()

            def body(pool, b, b0):
                T = T_(b0)
                pool.wait_ge(bank_free, b * NU + free(NPL - 1))
                if b0:
                    pool.tensor_copy(rwp[:, :, 0:1], rws[:]).then_inc(shift_sv, 1)
                    pool.wait_ge(shift_sv, 1)
                    pool.tensor_copy(rws[:], rwp[:, :, NSAMP:NSAMP + 1]).then_inc(shift_sv, 1)
                    pair_steps(b, b0, Pair(None, 0), None)
                    pool.wait_ge(s_shift, 16)
                else:
                    pool.wait_ge(y_st, b * (16 * KD))
                    pool.wait_ge(saved, b * 2)
                    settled(pool)
                    pool.tensor_copy(kvp[:, :, 0:CH], kvs[:, :, CH:2 * CH]).then_inc(lead, 1)
                    pool.tensor_copy(rwp[:, :, 0:1], rws[:]).then_inc(lead, 1)
                    pool.wait_ge(lead, b * 2)
                    settled(pool)
                with pool.Fori(0, NPAIR) as i:
                    pair_steps(b, b0, Pair(b * NPAIR + i, i * 128 + (CH if b0 else 0)), i)
                pool.tensor_copy(kvs[:], kvp[:, :, CH + T - 128:CH + T]).then_inc(saved, 1)
                pool.tensor_copy(rws[:], rwp[:, :, T:T + 1]).then_inc(saved, 1)
                for j in range(8):
                    dst, hi, src = (atl, ath, q) if j < 4 else (rwl, rwh, rwp)
                    pool.wait_ge(b_hi, b * 8 + (j + 1))
                    settled(pool)
                    pool.tensor_tensor(dst[:, j % 4, 0:T], src[:, j % 4, 0:T], hi[:, j % 4, 0:T],
                                       ALU.subtract).then_inc(b_lo, 1)
                with pool.Fori(0, KD) as d:
                    pool.wait_ge(m_hi, b * KD + d + 1)
                    settled(pool)
                    pool.tensor_tensor(ml[:, d, 0:T], acc[:, 0:T], mh[:, d, 0:T], ALU.subtract).then_inc(m_lo, 1)
                for d in range(KD):
                    pool.wait_ge(n2_hi, b * KD + (d + 1))
                    settled(pool)
                    pool.tensor_tensor(hl[:, d, 0:T], sq[d % 2][:, 0:T], hh[:, d, 0:T],
                                       ALU.subtract).then_inc(n2_lo, 1)
                for s, g in enumerate(GROUPS):
                    with pool.Fori(0, g) as i:
                        pool.wait_ge(f_hi, b * NFF + i + (sum(GROUPS[:s]) + 1))
                        settled(pool)
                        pool.tensor_tensor(fl[:, i, 0:T], acc[:, 0:T], fh[:, i, 0:T], ALU.subtract).then_inc(f_lo, 1)
                with pool.Fori(0, KD // 2) as i:
                    for p in range(2):
                        pool.wait_ge(n1_hi, b * KD + i * 2 + (p + KD + 1))
                        settled(pool)
                        pool.tensor_tensor(hl[:, i * 2 + p, 0:BT], nt[p][:, 0:BT], hh[:, i * 2 + p, 0:BT],
                                           ALU.subtract).then_inc(n1_lo, 1)

            pool.wait_ge(ld, LDALL)
            pool.memset(scratch[:, 0:1], 0.0).then_inc(m_lo, 1)
            pool.memset(scratch[:, 1:2], 0.0).then_inc(f_lo, 1)
            for d in range(KD):
                pool.wait_ge(n1_hi, d + 1)
                pool.tensor_tensor(hl[:, d, :], nt[d % 2][:], hh[:, d, :], ALU.subtract).then_inc(n1_lo, 1)
            blocks(pool, body)

        @block.vector
        def _(dve):
            def split(b, off, i):
                u, p = ring(b, off, i), off % 2
                dve.wait_ge(hi_done, u + 1)
                dve.tensor_tensor(wl[p][:], raw[p][:], wh[p][:], ALU.subtract).then_inc(lo_done, 1)

            def clear(s, sem_sum, wait):
                dve.wait_ge(*wait)
                dve.memset(s[:], 0.0).then_inc(sem_sum, 1)

            def add_sq(T, s, src, sem_sq, nth, sem_sum, count):
                dve.wait_ge(sem_sq, nth)
                dve.wait_ge(sem_sum, count)
                dve.tensor_tensor(s[:, 0:T], s[:, 0:T], src[:, 0:T], ALU.add).then_inc(sem_sum, 1)

            def scaled(T, out, src, c, d, r):
                return dve.scalar_tensor_tensor(out=out, in0=src, scalar=cst[:, c + d:c + d + 1],
                                                in1=r[:, 0:T], op0=ALU.mult, op1=ALU.mult)

            def pair_steps(b, b0, pr, i):
                step = Order(pr, "V")
                V, A, G, Tn = rw["V"], rw["A"], rw["G"], rw["T"]
                W, n = pr.w, pr.n

                def own(name):
                    dve.wait_ge(V, pr.at("V", name))

                def v4(t):
                    return t[:].rearrange("p a w -> p (a w)")[:, 0:4 * W].rearrange("p (a w) -> p a w", a=4)

                def v8(t):
                    return t[:].rearrange("p a w -> p (a w)")[:, 0:4 * W].rearrange("p (a w) -> p a w", w=CH)

                def fl(t):
                    return t[:].rearrange("p a w -> p (a w)")[:, 0:4 * W]

                xsf = xs[:].rearrange("p a w -> p (a w)")

                def xp(plane):
                    return xsf[:, plane * W:(plane + 4) * W]

                def ps(bank):
                    return PS[:, bank, 0:4 * W]

                def tt_(name, out, a, bb_, op):
                    step(name)
                    dve.tensor_tensor(out, a, bb_, op).then_inc(V, 1)

                def ts_(name, out, a, s1, s2, op0, op1=None):
                    step(name)
                    (dve.tensor_scalar(out, a, s1, s2, op0, op1) if op1 else
                     dve.tensor_scalar(out, a, s1, None, op0)).then_inc(V, 1)

                def rc_(name, out, a):
                    step(name)
                    dve.reciprocal(out, a).then_inc(V, 1)

                def stt_(name, out, a, s, bb_, op0, op1):
                    step(name)
                    dve.scalar_tensor_tensor(out=out, in0=a, scalar=s, in1=bb_, op0=op0, op1=op1).then_inc(V, 1)

                def q4(bank, width):
                    return PS[:, bank, 0:4 * width].rearrange("p (a w) -> p a w", a=4)

                def gates_recip(f):
                    u = ring(b, U_GA + f, i)
                    g_ = ga[:, i * 2 + f, 0:T_(b0)]
                    dve.wait_ge(ga_exp, b * KD + i * 2 + (f + 1))
                    settled(dve)
                    dve.tensor_scalar(g_, g_, 1.0, None, ALU.add).then_inc(bank_free, 1)
                    dve.wait_ge(bank_free, free(u))
                    settled(dve)
                    dve.reciprocal(g_, g_).then_inc(ga_done, 1)

                def soft(c):
                    m0, m1, m2 = mxs[:, 0, :], mxs[:, 1, :], mxs[:, 2, :]
                    dve.wait_ge(Tn, pr.at("T", f"s{c}"))
                    if c == 0 and not pr.sample:
                        dve.wait_ge(s_reset, 2)
                    if c:
                        dve.wait_ge(Tn, pr.at("T", "ptr0"))
                    stt_(f"sm{c}", sm[:], q4(2, 128), SCALE, kmask[:, c, :].unsqueeze(1).to_broadcast([128, 4, 128]),
                         ALU.mult, ALU.add)
                    own(f"sm{c}")
                    step(f"mx{c}")
                    dve.tensor_reduce(m0, sm[:], AX, ALU.max).then_inc(V, 1)
                    own(f"mx{c}")
                    tt_(f"mx2{c}", m0, m0, cst[:, C_SINK:C_SINK + 4], ALU.max)
                    own(f"mx2{c}")
                    tt_(f"sub{c}", sm[:], sm[:], m0.unsqueeze(2).to_broadcast([128, 4, 128]), ALU.subtract)
                    tt_(f"sk{c}", m1, cst[:, C_SINK:C_SINK + 4], m0, ALU.subtract)
                    dve.wait_ge(A, pr.at("A", f"es{c}"))
                    step(f"sum{c}")
                    dve.tensor_reduce(m2, sm[:], AX, ALU.add).then_inc(V, 1)
                    own(f"sum{c}")
                    tt_(f"den{c}", m2, m2, m1, ALU.add)
                    own(f"den{c}")
                    rc_(f"rec{c}", m2, m2)
                    own(f"rec{c}")
                    tt_(f"pn{c}", sm[:], sm[:], m2.unsqueeze(2).to_broadcast([128, 4, 128]), ALU.mult)

                soft(0)
                dw = xsf[0:64, 12 * W:13 * W]
                dg = xsf[:, 13 * W:14 * W]
                dve.wait_ge(A, pr.at("A", "et"))
                ts_("t1", dw, dw, 1.0, None, ALU.add)
                own("t1")
                rc_("t2", dw, dw)
                own("t2")
                ts_("t3", dw, dw, -2.0, 1.0, ALU.mult, ALU.add)
                dve.wait_ge(A, pr.at("A", "eg"))
                ts_("g1", dg, dg, 1.0, None, ALU.add)
                own("g1")
                rc_("g2", dg, dg)
                if not pr.sample:
                    split(b, U_GA + 1, i)
                dve.wait_ge(Tn, pr.at("T", "z"))
                tt_("z1", v4(zz), q4(4, W), cv(C_W0, 4, W), ALU.add)
                dve.wait_ge(Tn, pr.at("T", "a"))
                tt_("a1", v4(aa), q4(5, W), cv(C_A0, 4, W), ALU.add)
                ts_("n1", fl(pp), ps(7), 1e-24, None, ALU.max)
                dve.wait_ge(A, pr.at("A", "z2"))
                ts_("z3", fl(zz), fl(zz), 1.0, None, ALU.add)
                own("z3")
                rc_("z4", fl(zz), fl(zz))
                dve.wait_ge(A, pr.at("A", "a2"))
                ts_("a3", fl(aa), fl(aa), 1.0, None, ALU.add)
                own("a3")
                rc_("a4", fl(aa), fl(aa))
                own("z4")
                ts_("lw", fl(zz), fl(zz), -EXPM05, None, ALU.mult)
                own("lw")
                vm = vmask[:].unsqueeze(1).to_broadcast([128, 4, CH])
                if pr.sample:
                    tt_("lwm", v4(zz), v4(zz), vm, ALU.mult)
                    own("lwm")
                step("scan")
                dve.tensor_tensor_scan(fl(cc), scanm[:].rearrange("p a w -> p (a w)")[:, 0:4 * W], fl(zz), 0.0,
                                       ALU.mult, ALU.add).then_inc(V, 1)
                if not pr.sample:
                    gates_recip(0)
                stt_("kt1", v4(kt), v4(aa), -1.0, cv(C_KA, 4, W), ALU.add, ALU.mult)
                own("kt1")
                stt_("kt2", fl(kt), fl(kt), 1.0, xp(4), ALU.add, ALU.mult)
                if pr.sample:
                    own("kt2")
                    tt_("ktm", v4(kt), v4(kt), vm, ALU.mult)
                dve.wait_ge(G, pr.at("G", "kkn"))
                tt_("bb", fl(aa), fl(kk), fl(aa), ALU.mult)
                if pr.sample:
                    own("bb")
                    tt_("bbm", v4(aa), v4(aa), vm, ALU.mult)
                dve.wait_ge(A, pr.at("A", "ip"))
                own("bbm" if pr.sample else "bb")
                stt_("at", ra[:, 0:4 * n, 1, :], v8(kk), -1.0, v8(zz), ALU.mult, ALU.mult)
                tt_("rt", ra[:, 0:4 * n, 0, :], xp(0).rearrange("p (a w) -> p a w", w=CH), v8(pp), ALU.mult)
                step("pc")
                dve.tensor_copy(pcf[:, 0:4 * n], v8(pp)[:, :, CH - 1]).then_inc(V, 1)
                tt_("bt", bkk[:, 0:4 * n, 1, :], v8(aa), v8(ip), ALU.mult)
                tt_("ktl", bkk[:, 0:4 * n, 0, :], v8(kt), v8(ip), ALU.mult)
                tt_("bo1", v4(cc), xp(0).rearrange("p (a w) -> p a w", a=4), cv(C_RK, 4, W), ALU.mult)
                own("bo1")
                tt_("bo2", fl(cc), fl(cc), fl(kt), ALU.mult)
                if not pr.sample:
                    gates_recip(1)
                    split(b, U_GA + 2, i)
                    soft(1)
                dve.wait_ge(Tn, pr.at("T", "bo"))
                tt_("bv", fl(kt), ps(4), xp(8), ALU.mult)

                def q8(bank, r=slice(0, 128), c0=0, width=CH):
                    return PS[r, bank, c0:c0 + 4 * width].rearrange("p (a w) -> p a w", a=4)

                for c in pr.chs:
                    dve.wait_ge(Tn, pr.at("T", f"lm{c}"))
                    for par, name in enumerate(("E", "O")):
                        tt_(f"lm{name}{c}", lm[c][:, par], q4(4 + 2 * c + par, 128), mrep(M_LM, 4), ALU.mult)
                    for par, name in enumerate(("E", "O")):
                        r = half_rows(par)
                        tt_(f"yd{name}{c}", yd[c][r], q4(4 + 2 * c + par, 128)[r, :, CH:128],
                            mrep(M_YD, 4, 64 * par, 64 * par + 64, 0, 64), ALU.mult)
                for c in pr.chs:
                    dve.wait_ge(Tn, pr.at("T", f"xv{c}"))
                    tt_(f"xd{c}", xd[c][:], q8(4 + 2 * c), mrep(M_XD, 4, c0=0, c1=64), ALU.mult)
                    step(f"svE{c}")
                    dve.tensor_copy(sv[c][64:128, :, 0, :], q8(4 + 2 * c, slice(64, 128), 256)).then_inc(V, 1)
                    step(f"svO{c}")
                    dve.tensor_copy(sv[c][0:64, :, 1, :], q8(4 + 2 * c, slice(0, 64), 256)).then_inc(V, 1)

                def grow(name, st_, bank, first=None):
                    for c in pr.chs:
                        dve.wait_ge(Tn, pr.at("T", f"{st_}{c}"))
                        tt_(f"{name}{c}", pt[c][:], pt[c][:], q8(bank + 2 * c), ALU.add)

                grow("pt2", "s2_", 5)
                grow("pt3", "s3_", 5)
                grow("dt", "s4_", 4)
                grow("rr", "s7_", 5)
                grow("tt", "s8_", 4)
                for c in pr.chs:
                    b0_, b1_ = 4 + 2 * c, 5 + 2 * c
                    dve.wait_ge(Tn, pr.at("T", f"q0{c}"))
                    dve.wait_ge(A, pr.at("A", f"zl{c}"))
                    tt_(f"x{c}", yo[c][:], zl[c][:], q8(b1_), ALU.add)
                    dve.wait_ge(Tn, pr.at("T", f"sa{c}"))
                    step(f"saE{c}")
                    dve.tensor_copy(sv[c][0:64, :, 0, :], q8(b1_, slice(0, 64))).then_inc(V, 1)
                    step(f"saO{c}")
                    dve.tensor_copy(sv[c][64:128, :, 1, :], q8(b1_, slice(64, 128))).then_inc(V, 1)
                    dve.wait_ge(Tn, pr.at("T", f"ds{c}"))
                    tt_(f"st1{c}", st[:], st[:], q8(b1_), ALU.add)
                    own(f"st1{c}")
                    pcv = pcf[:, 0:4 * n].rearrange("p (a c) -> p a c", c=n)[:, :, c:c + 1].to_broadcast([128, 4, CH])
                    tt_(f"st2{c}", st[:], st[:], pcv, ALU.mult)
                    dve.wait_ge(Tn, pr.at("T", f"o2{c}"))
                    o_ = v4(ip)[:, :, CH * c:CH * c + CH]
                    tt_(f"o{c}", o_, o_, q8(b0_), ALU.add)
                dve.wait_ge(Tn, pr.at("T", "mean"))
                tt_("oc", fl(ip), fl(ip), ps(4), ALU.subtract)
                dve.wait_ge(A, pr.at("A", "v2"))
                tt_("on", fl(ip), fl(ip), fl(zz), ALU.mult)
                step("km")
                dve.memset(kmask[:], 0.0).then_inc(V, 1)
                step.end()

            pcf = pcol[:].rearrange("p a c -> p (a c)")

            def body(dve, b, b0):
                T = T_(b0)
                for dest, k, lead_, first in ((q, 4, 0, 0), (kvp, 2, CH, 4), (rwp, NRW, 1, 6)):
                    with dve.Fori(0, k // 2) as i:
                        for p in range(2):
                            split(b, first + p + 1, i)
                            dve.wait_ge(mm_done, mmd(ring(b, first + p, i)))
                            settled(dve)
                            dve.tensor_copy(view(dest[:, i * 2 + p, lead_:lead_ + T], b0),
                                            psv(2 * p, b0)).then_inc(bank_free, 1)
                if b0:
                    pair_steps(b, b0, Pair(None, 0), None)
                    dve.wait_ge(s_sstate, 16)
                    dve.memset(st[:], 0.0).then_inc(s_reset, 1)
                    dve.wait_ge(rw["V"], Pair(None, 0).all("V"))
                    dve.memset(kmask[:, 0, 0:CH], NEG).then_inc(s_reset, 1)
                with dve.Fori(0, NPAIR) as i:
                    pair_steps(b, b0, Pair(b * NPAIR + i, i * 128 + (CH if b0 else 0)), i)
                with dve.Fori(0, KD) as d:
                    split(b, U_BR + 1, d)
                    dve.wait_ge(gb_exp, b * KD + d + 1)
                    dve.tensor_scalar(e1[:, 0:T], e1[:, 0:T], 1.0, None, ALU.add).then_inc(bank_free, 1)
                    dve.wait_ge(bank_free, free(ring(b, U_BR, d)))
                    dve.reciprocal(e1[:, 0:T], e1[:, 0:T]).then_inc(v_own, 1)
                    split(b, U_BR + 2, d)
                    own = (b * KD + d) * 2
                    dve.wait_ge(mm_done, mmd(ring(b, U_BR + 1, d)))
                    dve.wait_ge(ga_done, b * KD + KD)
                    settled(dve)
                    dve.tensor_tensor(view(e2[:, 0:T], b0), view(ga[:, d, 0:T], b0), psv(4, b0),
                                      ALU.mult).then_inc(v_own, 1)
                    dve.wait_ge(v_own, own + 1)
                    dve.tensor_tensor(view(e1[:, 0:T], b0), view(e1[:, 0:T], b0), psv(6, b0),
                                      ALU.mult).then_inc(bank_free, 1)
                    dve.wait_ge(v_own, own + 2)
                    dve.wait_ge(bank_free, free(ring(b, U_BR + 1, d)))
                    dve.wait_ge(m_lo, b * KD + d + 1)
                    settled(dve)
                    dve.tensor_tensor(acc[:, 0:T], e1[:, 0:T], e2[:, 0:T], ALU.add).then_inc(m_sum, 1)

                def residual(off, i, p):
                    split(b, off + 1, i)
                    dve.wait_ge(mm_done, mmd(ring(b, off, i)))
                    dve.wait_ge(xres_ld, b * 16 + 16)
                    settled(dve)
                    xr = xres[:, i * 2 + p, 0:T]
                    dve.tensor_tensor(view(xr, b0), view(xr, b0), psv(2 * p, b0), ALU.add).then_inc(bank_free, 1)

                clear(acc, n2_sum, (m_lo, b * KD + (KD + 1)))
                with dve.Fori(0, KD // 2) as i:
                    for p in range(2):
                        residual(U_WO + p, i, p)
                        add_sq(T, acc, sq[p], n2_sq, b * (2 * KD) + i * 2 + (p + 1), n2_sum, summed(b * 2, i * 2 + p))
                for d in range(KD):
                    dve.wait_ge(n2_rs, b * 4 + 2)
                    if d >= 2:
                        dve.wait_ge(n2_lo, b * KD + (d - 1))
                    settled(dve)
                    scaled(T, sq[d % 2][:, 0:T], xres[:, d, 0:T], C_N2, d, rs).then_inc(n2_t, 1)
                for s, g in enumerate(GROUPS):
                    with dve.Fori(0, g) as i:
                        f = b * NFF + i + sum(GROUPS[:s])
                        split(b, U_F[s] + 1, i)
                        own = b * (2 * NFF) + i * 2 + (2 * sum(GROUPS[:s]))
                        dve.wait_ge(f_exp, f + 1)
                        dve.tensor_scalar(e1[:, 0:T], e1[:, 0:T], 1.0, None, ALU.add).then_inc(f_own, 1)
                        dve.wait_ge(f_own, own + 1)
                        dve.reciprocal(e1[:, 0:T], e1[:, 0:T]).then_inc(f_own, 1)
                        dve.wait_ge(f_own, own + 2)
                        dve.tensor_tensor(view(e2[:, 0:T], b0), view(e1[:, 0:T], b0), psv(0, b0),
                                          ALU.mult).then_inc(bank_free, 1)
                        split(b, U_F[s] + 2, i)
                        dve.wait_ge(mm_done, mmd(ring(b, U_F[s] + 1, i)))
                        dve.wait_ge(bank_free, free(ring(b, U_F[s], i)))
                        dve.wait_ge(f_lo, f + 1)
                        dve.tensor_tensor(view(acc[:, 0:T], b0), view(e2[:, 0:T], b0), psv(2, b0),
                                          ALU.mult).then_inc(bank_free, 1)
                    if s == 1:
                        clear(nsum, n1_sum, (n2_rs, b * 4 + 2))
                    if s == 2:
                        clear(acc, n2_sum, (f_lo, b * NFF + (NFF + 1)))
                    for i in range(KD // 2) if s == 2 else [None]:
                        with ExitStack() as loop:
                            if s != 2:
                                i = loop.enter_context(dve.Fori(0, KD // 2))
                            down(b, b0, T, s, g, i, residual)
                for d in range(KD):
                    dve.wait_ge(n2_rs, b * 4 + 4)
                    scaled(T, xres[:, d, 0:T], xres[:, d, 0:T], C_NF, d, rs).then_inc(y_done, 1)

            def down(b, b0, T, s, g, i, residual):
                for p in range(2):
                    if s == 2:
                        dve.wait_ge(n1_rs, b * 2 + 4)
                        dve.wait_ge(n1_lo, b * KD + (i * 2 + p + KD - 1))
                        settled(dve)
                        scaled(BT, nt[p][:, 0:BT], xin[:, i * 2 + p, 0:BT], C_N1, i * 2 + p, nrs).then_inc(n1_t, 1)
                    residual(U_F[s] + 2 * g + p, i, p)
                    if s == 1:
                        add_sq(BT, nsum, nt[p], n1_sq, b * KD + i * 2 + (p + KD + 1),
                               n1_sum, b * (KD + 1) + i * 2 + (p + KD + 2))
                    if s == 2:
                        add_sq(T, acc, sq[p], n2_sq, b * (2 * KD) + (i * 2 + p + KD + 1),
                               n2_sum, summed(b * 2 + 1, i * 2 + p))

            for c, value in enumerate((RMS_EPS, GN_EPS, 10 * LN2)):
                dve.memset(bias[:, c:c + 1], value).then_inc(ini, 1)
            dve.memset(scanm[:], 1.0).then_inc(ini, 1)
            dve.memset(vmask[:, 0:NSAMP], 1.0).then_inc(ini, 1)
            dve.memset(vmask[:, NSAMP:CH], 0.0).then_inc(m_sum, 1)
            dve.memset(kmask[:], 0.0).then_inc(ini, 1)
            dve.wait_ge(ini, 6)
            dve.memset(scanm[:, :, 0:1], 0.0).then_inc(bank_free, 2)
            dve.memset(kmask[:, 0, CH + NSAMP:128], NEG).then_inc(n2_sum, 1)
            dve.memset(nsum[:], 0.0).then_inc(n1_sum, 1)
            for d in range(KD):
                add_sq(MT, nsum, nt[d % 2], n1_sq, d + 1, n1_sum, d + 1)
            split(0, 0, 0)
            dve.wait_ge(n1_rs, 2)
            for d in range(KD):
                if d >= 2:
                    dve.wait_ge(n1_lo, d - 1)
                scaled(MT, nt[d % 2][:], xin[:, d, :], C_N1, d, nrs).then_inc(n1_t, 1)
            dve.wait_ge(bank_free, 2)
            dve.wait_ge(m_sum, 1)
            dve.wait_ge(n2_sum, 1)
            blocks(dve, body)


def kernel(**inputs):
    import numpy as np
    import concourse.bacc as bacc
    from concourse.bass_utils import run_bass_kernel_spmd

    a = {name: np.asarray(v) for name, v in inputs.items()}
    f32 = np.float32

    def planes(m):
        return m.reshape(m.shape[0], -1, 128).transpose(2, 1, 0)

    x = np.zeros((128, KD, NTOK + BT), f32)
    x[:, :, 0:NSAMP] = planes(a["x_sample"][0])
    x[:, :, CH:NTOK] = planes(a["x_prompt"][0])

    heads = [h for j in range(4) for h in (j, j + 4)]
    q_rows = np.concatenate([np.arange(64 * h, 64 * h + 64) for h in heads])
    w_in, w_branch = a["w_in"][0], a["w_branch"][0]
    gates = w_in[:, (NPL * 128):]
    units = [w_in[:, q_rows][:, 128 * j:128 * j + 128] for j in range(4)]
    units += [w_in[:, 128 * j:128 * j + 128] for j in range(4, NPL)]
    units += [gates[:, 128 * j:128 * j + 128] for j in range(KD)]
    both = np.concatenate([w_branch[0][q_rows], w_branch[1]])
    for d in range(KD):
        c = slice(128 * d, 128 * d + 128)
        units += [gates[:, D:][:, c], both[:, c]]
    units += [a["w_out"][0][:, 128 * j:128 * j + 128] for j in range(KD)]
    first = 0
    for g in GROUPS:
        for j in range(first, first + g):
            c = slice(128 * j, 128 * j + 128)
            units += [a["w_ffn_gate"][0][:, c], a["w_ffn_up"][0][:, c]]
        for j in range(KD):
            part = np.zeros((D, 128), f32)
            part[0:128 * g] = a["w_ffn_down"][0][128 * first:128 * (first + g), 128 * j:128 * j + 128]
            units.append(part)
        first += g
    w = np.stack(units).reshape(NU, KD, 128, 128).transpose(0, 2, 1, 3).reshape(NU, 128, WU)

    def cols(v):
        return v.reshape(-1, 128).T

    sinks = np.repeat(a["attn_sinks"][0].reshape(2, 4), 64, axis=0)
    col = np.concatenate([cols(a[n][0]) for n in ("mu_shift", "w0", "a0", "k_k", "k_a")]
                         + [cols(a["r_k"][0].reshape(-1)), cols(a["lnx_g"][0]), cols(a["lnx_b"][0]),
                            cols(a["norm1_g"][0]), cols(a["norm2_g"][0]), cols(a["final_norm_g"]), sinks], axis=1)

    p, f = np.arange(128)[:, None], np.arange(128)[None, :]
    s, t = p % 64, f % 64
    mats = np.zeros((128, NMAT, 128), f32)
    mats[:, M_ID] = p == f
    mats[:, M_ONE] = 1
    mats[:, M_HEAD] = p // 64 == f // 64
    mats[:, M_MEAN] = (p // 64 == f // 64) / 64.0
    mats[:, M_LM] = np.where(f < 64, s <= t, s < t)
    mats[:, M_YD] = np.where(f < 64, s // 16 == t // 16, s // 16 != t // 16) & (s < t)
    mats[:, M_XD] = np.where(f < 64, (s // 16 == t // 16) & (s > t), s == t)

    loras = np.zeros((128, 2, 512), f32)
    loras[0:64, 0], loras[64:128, 0], loras[:, 1] = a["w2"][0], a["a2"][0], a["g2"][0]

    def kv_in(m):
        return m.reshape(128, 128).T

    arrays = {
        "x": x, "w": w, "col": col, "mats": mats, "loras": loras,
        "kv_cache": np.stack([kv_in(a["cache_attn_k"][0, 0]), kv_in(a["cache_attn_v"][0, 0])], axis=1),
        "st_in": a["state_rwkv"][0, 0].reshape(4, 2, 64, 64).transpose(1, 3, 0, 2).reshape(128, 4, 64),
        "shift_in": a["state_shift"][0, 0].reshape(NRW, 128).T[:, :, None],
    }
    arrays = {n: np.ascontiguousarray(v) for n, v in arrays.items()}
    outs = {"y": (128, KD, NTOK), "st_s": (128, 4, 64), "st_p": (128, 4, 64), "shift_s": (128, NRW, 1),
            "shift_p": (128, NRW, 1), "kv_s": (128, 2, 128), "kv_p": (128, 2, 128)}
    nc = bacc.Bacc("TRN2", target_bir_lowering=False, num_devices=1)
    args = [nc.dram_tensor(n, v.shape, F32, kind="ExternalInput").ap() for n, v in arrays.items()]
    args += [nc.dram_tensor(n, s_, F32, kind="ExternalOutput").ap() for n, s_ in outs.items()]
    hybrid_layer(nc, *args)
    r = run_bass_kernel_spmd(nc, [arrays], core_ids=[0]).results[0]

    y = r["y"].transpose(2, 1, 0).reshape(NTOK, D)

    def kv_out(m, which):
        return m[:, which].T.reshape(1, 1, 128, 2, 64)

    def state_out(m):
        return m.reshape(2, 64, 4, 64).transpose(2, 0, 3, 1).reshape(1, 1, 8, 64, 64)

    def shift_out(m):
        return m[:, :, 0].T.reshape(1, 1, 1, NRW * 128)

    return (y[None, CH:], y[None, 0:NSAMP],
            kv_out(r["kv_p"], 0), kv_out(r["kv_p"], 1), state_out(r["st_p"]), shift_out(r["shift_p"]),
            kv_out(r["kv_s"], 0), kv_out(r["kv_s"], 1), state_out(r["st_s"]), shift_out(r["shift_s"]))
```

```python
from contextlib import ExitStack

import concourse.bass as bass
from concourse import mybir

F32 = mybir.dt.float32
F32R = mybir.dt.float32r
ALU = mybir.AluOpType
ACT = mybir.ActivationFunctionType
AX = mybir.AxisListType.X

D = 1024
CH = 64
NSAMP = 32
KD = D // 128
DFF = 2816
NFF = DFF // 128
GROUPS = (8, 8, 6)
NRW = 14
NPL = 6 + NRW
BT = 512
NB = 4
MT = BT + CH
NPAIR = BT // 128
NTOK = CH + NB * BT
U_GA = NPL
U_BR = U_GA + KD
U_WO = U_BR + 2 * KD
U_F = [U_WO + KD + sum(2 * g + KD for g in GROUPS[:i]) for i in range(len(GROUPS))]
NU = U_F[-1] + 2 * GROUPS[-1] + KD
WU = KD * 128
SCALE = 64 ** -0.5
EXPM05 = 0.6065306597126334
LN2 = 0.6931471805599453
RMS_EPS = 1e-6
GN_EPS = 64e-5
C_MU, C_W0, C_A0, C_KK, C_KA, C_RK, C_LG, C_LB = 0, 14, 18, 22, 26, 30, 34, 38
C_N1, C_N2, C_NF, C_SINK, NCOL = 42, 50, 58, 66, 70
M_ID, M_ONE, M_HEAD, M_MEAN, M_LM, M_YD, M_XD, NMAT = 0, 1, 2, 3, 4, 5, 6, 7
NEG = -1e30


def steps(engine, sample):
    chs = (0,) if sample else (0, 1)

    def each(*names):
        return [f"{n}{c}" for c in chs for n in names]

    def by(*names):
        return [f"{n}{c}" for n in names for c in chs]

    if engine == "V":
        s = by("sm") + ["mx", "mx2", "sub", "sk", "z1", "a1", "n1"]
        s += ["lwm"] * sample + ["scan", "kt1", "kt2"] + ["ktm"] * sample
        s += ["sum", "den", "rec", "pn", "bb"] + ["bbm"] * sample
        s += ["at", "rt", "pc", "btE", "btO", "ktE", "ktO", "bv"]
        s += each("lmE", "lmO", "ydE", "ydO") + each("xd", "svE", "svO")
        s += by("pt2", "pt3", "dt", "rr", "tt")
        s += each("x", "saE", "saO", "st1", "st2", "o") + ["oc", "on", "lg", "ob", "gate", "km"]
        return s
    if engine == "A":
        s = ["et", "eg", "ksq", "vt", "z2", "a2", "ex", "es", "gcp", "n2", "n3", "pm", "p", "ip", "ptr", "at"]
        return s + by("tok", "xy2", "xy4", "x8", "d", "zl", "g", "h") + each("o1") + ["osq", "v1", "v2"]
    if engine == "G":
        s = ["xs1", "xs2", "xs3", "kk", "qb", "kvb", "cm", "kkn", "bo1", "bo2"]
        return s + each("yoE", "yoO", "pt1") + ["lb"]
    s = ["s", "vt", "z", "a", "kn", "g", "ptr", "pv", "bo"]
    s += by("lm") + each("xv", "tok") + by("s1_", "s2_", "s3_", "s4_") + each("s5_", "lv") + by("s6_", "s7_", "s8_")
    return s + each("q0", "o1", "sa", "ds", "o2") + ["mean", "var"]


class Pair:

    def __init__(self, g, tok):
        self.sample = g is None
        self.tok, self.chs = tok, (0,) if self.sample else (0, 1)
        self.w = CH * len(self.chs)
        self.n = len(self.chs)
        self.names = {e: steps(e, self.sample) for e in "VAGT"}
        if self.sample:
            self.base = dict.fromkeys("VAGT", 0)
        else:
            self.base = {e: g * len(steps(e, False)) + len(steps(e, True)) for e in "VAGT"}

    def at(self, engine, name):
        return self.base[engine] + (self.names[engine].index(name) + 1)

    def all(self, engine):
        return self.base[engine] + len(self.names[engine])


def back(engine, name):
    names = steps(engine, True)
    return len(names) - 1 - names.index(name)


class Order:

    def __init__(self, pair, engine):
        self.names, self.n = pair.names[engine], 0

    def __call__(self, name):
        assert self.names[self.n] == name, (self.names[self.n], name)
        self.n += 1

    def end(self):
        assert self.n == len(self.names), self.names[self.n]


def hybrid_layer(nc, x, w, col, mats, loras, kv_cache, st_in, shift_in,
                 y, st_s, st_p, shift_s, shift_p, kv_s, kv_p):
    with ExitStack() as ctx:
        def sem(name):
            return ctx.enter_context(nc.semaphore(name))

        cursor = [17 * 1024]

        def place(name, shape, dt=F32, at=None):
            size = 4
            for n in shape[1:]:
                size *= n
            if at is None:
                at = cursor[0]
                cursor[0] += (size + 31) // 32 * 32
            return nc.alloc_sbuf_tensor_at(name, shape, dt, offset=at), at

        def new(name, shape, dt=F32):
            return place(name, shape, dt)[0]

        PLANE = 4 * MT
        hh, hl = new("hh", [128, KD, MT], F32R), new("hl", [128, KD, MT], F32R)
        at_p = cursor[0]
        q = new("q", [128, 4, MT])
        kvp = new("kvp", [128, 2, CH + MT])
        rwp = new("rwp", [128, NRW, 1 + MT])
        assert cursor[0] - at_p >= 16 * PLANE
        mh, _ = place("mh", [128, KD, MT], F32R, at_p)
        ml, _ = place("ml", [128, KD, MT], F32R, at_p + KD * PLANE)
        nsum, nrs, nt0, nt1 = (place(n, [128, MT], F32, at_p + (16 + i) * PLANE)[0]
                               for i, n in enumerate(("nsum", "nrs", "nt0", "nt1")))
        nt = [nt0, nt1]
        assert cursor[0] - at_p >= 20 * PLANE
        ga, at_ga = place("ga", [128, KD, MT])
        xin, _ = place("xin", [128, KD, MT], F32, at_ga)
        raw = [new(f"raw{i}", [128, WU]) for i in range(2)]
        wh = [new(f"wh{i}", [128, WU], F32R) for i in range(2)]
        wl = [new(f"wl{i}", [128, WU], F32R) for i in range(2)]
        cst = new("cst", [128, NCOL])
        mat = new("mat", [128, NMAT, 128])
        lora = new("lora", [128, 2, 512])
        bias = new("bias", [128, 4])
        scratch = new("scratch", [128, 2])
        scanm = new("scanm", [128, 8, CH])
        kvs = new("kvs", [128, 2, 128])
        rws = new("rws", [128, NRW, 1])
        vmask = new("vmask", [128, CH])
        kmask = new("kmask", [128, 2, 128])
        st = new("st", [128, 4, CH])
        pcol = new("pcol", [128, 4, 2])
        at_s = cursor[0]
        xs = new("xs", [128, NRW, 128])
        kk, zz, aa, gg, cc, pp, ip, kt = (new(n, [128, 4, 128]) for n in "kk_ zz_ aa_ gg_ cc_ pp_ ip_ kt_".split())
        ra = new("ra", [128, 8, 2, CH])
        bkk = new("bkk", [128, 8, 2, CH])
        at_lm = cursor[0]
        lm = [new(f"lm{c}", [128, 2, 4, 128]) for c in range(2)]
        tk = [new(f"tk{c}", [128, 4, 2, CH]) for c in range(2)]
        at_end = cursor[0]
        sv = [new(f"sv{c}", [128, 4, 2, CH]) for c in range(2)]
        yd, yo, xd, pt, zl = ([new(f"{n}{c}", [128, 4, CH]) for c in range(2)] for n in ("yd", "yo", "xd", "pt", "zl"))
        xy = [new(f"xy{c}", [128, 2, 4, CH]) for c in range(2)]
        at_xy4 = cursor[0]
        xy4 = [new(f"xyb{c}", [128, 2, 4, CH]) for c in range(2)]
        at_a = [at_lm]

        def attn(name, shape):
            t, a = place(name, shape, F32, at_a[0])
            size = 4
            for n in shape[1:]:
                size *= n
            at_a[0] = a + size
            return t

        sm = attn("sm", [128, 2, 4, 128])
        ptk = attn("ptk", [128, 2, 4, 128])
        vtk = attn("vtk", [128, 2, 128])
        mxs = attn("mxs", [128, 3, 8])
        assert at_a[0] <= at_end
        at_a[0] = at_xy4
        qb = attn("qb", [128, 4, 128])
        kvb = attn("kvb", [128, 2, CH + 128])
        assert at_a[0] <= at_xy4 + 2048 * 2
        at_d = [at_s]

        def dense(name, shape, dt=F32):
            t, a = place(name, shape, dt, at_d[0])
            size = 4
            for n in shape[1:]:
                size *= n
            at_d[0] = a + size
            return t

        ath, atl, rwh, rwl = (dense(n, [128, 4, MT], F32R) for n in ("ath", "atl", "rwh", "rwl"))
        fh, _ = place("fh", [128, KD, MT], F32R, at_s)
        fl, _ = place("fl", [128, KD, MT], F32R, at_s + KD * PLANE)
        xres = dense("xres", [128, KD, MT])
        sq = [dense(f"sq{i}", [128, MT]) for i in range(2)]
        acc, rs, e1, e2 = (dense(n, [128, MT]) for n in ("acc", "rs", "e1", "e2"))
        cursor[0] = max(cursor[0], at_d[0])
        assert cursor[0] <= nc.sbuf_usable_end, cursor[0]
        PS = ctx.enter_context(nc.psum_tensor("PS", [128, 8, 512], F32))

        shift_sv = sem("shift_sv")
        ini = sem("ini")
        xin_ld = sem("xin_ld")
        xres_ld = sem("xres_ld")
        w_ld = [sem(f"w_ld{i}") for i in range(2)]
        hi_done, lo_done = sem("hi_done"), sem("lo_done")
        mm_done = sem("mm_done")
        bank_free = sem("bank_free")
        gates = sem("gates")
        v_own = sem("v_own")
        rw = {"V": sem("dve_steps"), "A": sem("act_steps"), "G": sem("pool_steps"), "T": sem("pe_steps")}
        b_hi, b_lo = sem("b_hi"), sem("b_lo")
        m_sum, m_hi, m_lo = sem("m_sum"), sem("m_hi"), sem("m_lo")
        n1_sq, n1_sum, n1_ms, n1_rs = sem("n1_sq"), sem("n1_sum"), sem("n1_ms"), sem("n1_rs")
        n1_t, n1_hi, n1_lo = sem("n1_t"), sem("n1_hi"), sem("n1_lo")
        n2_sq, n2_sum, n2_ms, n2_rs = sem("n2_sq"), sem("n2_sum"), sem("n2_ms"), sem("n2_rs")
        n2_t, n2_hi, n2_lo = sem("n2_t"), sem("n2_hi"), sem("n2_lo")
        y_done, y_st = sem("y_done"), sem("y_st")
        f_hi, f_lo = sem("f_hi"), sem("f_lo")
        saved, lead = sem("saved"), sem("lead")
        s_reset = sem("s_reset")
        s_shift, s_sstate, s_out = sem("s_shift"), sem("s_sstate"), sem("s_out")

        ld = sem("ld")
        passed = sem("passed")

        LDALL = 16 * 6
        block = ctx.enter_context(nc.Block())

        def half(b0):
            return (2, MT // 2) if b0 else (1, BT)

        def view(ap, b0):
            h, n = half(b0)
            return ap.rearrange("p (h n) -> p h n", h=h)

        def psv(bank, b0):
            h, n = half(b0)
            return PS[:, bank:bank + h, 0:n]

        def T_(b0):
            return MT if b0 else BT

        def cv(c, n, width):
            return cst[:, c:c + n].unsqueeze(2).to_broadcast([128, n, width])

        def mrep(m, n, p0=0, p1=128, c0=0, c1=128):
            return mat[p0:p1, m, c0:c1].unsqueeze(1).to_broadcast([p1 - p0, n, c1 - c0])

        def mmd(u):
            return u + 3

        def free(u):
            return u + 3

        def summed(m, j):
            return m * (KD + 1) + (j + 2)

        def settled(eng):
            eng.sem_inc(passed, 1)

        def blocks(eng, body):
            body(eng, 0, True)
            with eng.Fori(1, NB) as b:
                body(eng, b, False)

        def ring(b, off, i=0):
            return b * NU + i * 2 + off

        def landed(b, off, i=0):
            return (b * (NU // 2) + i + (off // 2 + 1)) * 16

        @block.sync
        def _(sp):
            sp.dma_start(xin[:], x[:, :, 0:MT]).then_inc(xin_ld, 16)
            sp.dma_start(cst[:], col).then_inc(ld, 16)
            sp.dma_start(mat[:], mats).then_inc(ld, 16)
            sp.dma_start(lora[:], loras).then_inc(ld, 16)
            sp.dma_start(kvp[:, :, 0:CH], kv_cache[:, :, CH:2 * CH]).then_inc(ld, 16)
            sp.dma_start(st[:], st_in).then_inc(ld, 16)
            sp.dma_start(rws[:], shift_in).then_inc(ld, 16)
            sp.dma_start(kv_s[:, :, 0:128 - NSAMP], kv_cache[:, :, NSAMP:128]).then_inc(s_out, 16)

            def load_units(b, off, n):
                with sp.Fori(0, n // 2) as i:
                    for p in range(2):
                        sp.wait_ge(lo_done, ring(b, off + p - 1, i))
                        settled(sp)
                        sp.dma_start(raw[p][:], w[i * 2 + (off + p)]).then_inc(w_ld[p], 16)

            def body(sp, b, b0):
                if b0:
                    for p in range(2):
                        sp.dma_start(raw[p][:], w[p]).then_inc(w_ld[p], 16)
                    load_units(b, 2, NPL)
                    sp.wait_ge(bank_free, free(NPL - 1))
                    sp.wait_ge(shift_sv, 2)
                    sp.dma_start(shift_s, rws[:]).then_inc(s_shift, 16)
                    sp.dma_start(kv_s[:, :, 128 - NSAMP:128], kvp[:, :, CH:CH + NSAMP]).then_inc(s_out, 16)
                    sp.wait_ge(rw["V"], Pair(None, 0).at("V", "st20"))
                    sp.dma_start(st_s, st[:]).then_inc(s_sstate, 16)
                    load_units(b, NPL + 2, U_BR - NPL)
                else:
                    load_units(b, 0, U_BR + 2)
                sp.wait_ge(b_lo, b * 8 + 8)
                settled(sp)
                T = T_(b0)
                src = x[:, :, 0:MT] if b0 else x[:, :, bass.ds(b * BT + CH, BT)]
                sp.dma_start(xres[:, :, 0:T], src).then_inc(xres_ld, 16)
                load_units(b, U_BR + 2, U_F[0] - U_BR)
                sp.wait_ge(m_lo, b * KD + (KD + 1))
                settled(sp)
                sp.dma_start(xin[:, :, 0:BT], x[:, :, bass.ds(b * BT + MT, BT)]).then_inc(xin_ld, 16)
                load_units(b, U_F[0] + 2, NU - U_F[0] - 2)

            blocks(sp, body)
            sp.wait_ge(lo_done, NB * NU - 1)
            sp.dma_start(raw[0][:], w[0]).then_inc(w_ld[0], 16)
            sp.wait_ge(rw["V"], Pair(NB * NPAIR - 1, 0).all("V"))
            sp.dma_start(st_p, st[:]).then_inc(s_out, 16)
            sp.wait_ge(saved, 2 * NB)
            sp.dma_start(shift_p, rws[:]).then_inc(s_out, 16)
            sp.dma_start(kv_p, kvs[:]).then_inc(s_out, 16)
            sp.wait_ge(s_out, 16 * 5)
            sp.wait_ge(s_shift, 16)
            sp.wait_ge(s_sstate, 16)
            sp.wait_ge(y_st, 16 * KD * NB)

        def half_rows(par):
            return slice(64 * par, 64 * par + 64)

        @block.tensor
        def _(pe):
            def unit(b, b0, off, i, mh_, ml_, bank, back, planes=range(KD), k0=0, wait_k=None, only=None):
                u, p = ring(b, off, i), off % 2
                if only is None or k0 in only:
                    pe.wait_ge(hi_done, u + 1)
                    pe.wait_ge(lo_done, u + 1)
                    pe.wait_ge(bank_free, u + (3 - back))
                h, n = half(b0)
                for k in planes if only is None else only:
                    if wait_k:
                        pe.wait_ge(*wait_k(k))
                    cols = slice(128 * k, 128 * k + 128)
                    for a, (wt, mv) in enumerate(((wh[p], mh_), (wh[p], ml_), (wl[p], mh_))):
                        for f in range(h):
                            mm = pe.matmul(PS[:, bank + f, 0:n], wt[:, cols], mv[:, k - k0, f * n:f * n + n],
                                           start=(k == k0 and a == 0), stop=(k == planes[-1] and a == 2))
                return mm

            def norm_sum(b0, s, bank):
                h, n = half(b0)
                for f in range(h):
                    mm = pe.matmul(PS[:, bank + f, 0:n], mat[:, M_ONE], s[:, f * n:f * n + n], start=True, stop=True)
                return mm

            def pair_steps(b, b0, pr, i):
                step = Order(pr, "T")
                V, A, G = rw["V"], rw["A"], rw["G"]
                done = rw["T"]
                W, n = pr.w, pr.n

                def flat(t):
                    return t[:].rearrange("p a w -> p (a w)")[:, 0:4 * W]

                xsf = xs[:].rearrange("p a w -> p (a w)")

                def xsl(plane, a=0, z=None):
                    return xsf[:, plane * W + a:plane * W + (W if z is None else z)]

                def warm(k=2):
                    for _ in range(k):
                        pe.matmul(PS[:, 3, 0:128], mat[:, M_ONE], mat[:, M_ONE], start=True, stop=True)

                def filler(f, first=0, last=KD):
                    if pr.sample:
                        return
                    mm = unit(b, b0, U_GA + f, i, hh, hl, 0, 1, only=range(first, last))
                    if last == KD:
                        mm.then_inc(mm_done, 1)

                pe.wait_ge(G, pr.at("G", "kvb"))
                pe.wait_ge(bank_free, b * NU + free(NPL - 1))
                settled(pe)
                for c in pr.chs:
                    for j in range(4):
                        for kv in range(2):
                            r = half_rows(kv)
                            mm = pe.matmul(PS[r, 2 + c, 128 * j:128 * j + 128], qb[r, j, CH * c:CH * c + CH],
                                           kvb[r, 0, CH * c:CH * c + 128], start=True, stop=True)
                step("s")
                mm.then_inc(done, 1)
                for c in pr.chs:
                    mm = pe.transpose(PS[:, 6, 128 * c:128 * c + 128], kvb[:, 1, CH * c:CH * c + 128], mat[:, M_ID])
                step("vt")
                mm.then_inc(done, 1)
                for name, bank, r, m, plane in (("z", 4, slice(0, 64), 0, 12), ("a", 5, slice(64, 128), 0, 12),
                                                ("kn", 7, None, 0, 0), ("g", 6, slice(0, 128), 1, 13)):
                    pe.wait_ge(A, pr.at("A", {"z": "et", "a": "et", "kn": "ksq", "g": "vt"}[name]))
                    settled(pe)
                    step(name)
                    if name == "kn":
                        pe.matmul(PS[:, bank, 0:4 * W], mat[:, M_HEAD], flat(pp), start=True, stop=True).then_inc(done, 1)
                        continue
                    for j in range(4):
                        mm = pe.matmul(PS[:, bank, W * j:W * j + W], lora[r, m, 128 * j:128 * j + 128],
                                       xsf[r, plane * W:plane * W + W], start=True, stop=True)
                    mm.then_inc(done, 1)
                filler(0)
                filler(1, 0, 3)
                pe.wait_ge(V, pr.at("V", "pn"))
                settled(pe)
                for c in pr.chs:
                    for j in range(4):
                        mm = pe.transpose(PS[:, 2 + c, 128 * j:128 * j + 128], sm[:, c, j, :], mat[:, M_ID])
                step("ptr")
                mm.then_inc(done, 1)
                filler(1, 3, 5)
                pe.wait_ge(A, pr.at("A", "ptr"))
                settled(pe)
                for c in pr.chs:
                    for kv in range(2):
                        r = half_rows(kv)
                        out = PS[r, 7, 256 * c:256 * c + 256].rearrange("p (a w) -> p a w", a=4)
                        mm = pe.matmul(out, vtk[:, c, r], ptk[:, c, :, r], start=True, stop=True)
                step("pv")
                mm.then_inc(done, 1)
                filler(1, 5, 7)
                pe.wait_ge(G, pr.at("G", "bo2"))
                settled(pe)
                step("bo")
                pe.matmul(PS[:, 4, 0:4 * W], mat[:, M_HEAD], flat(cc), start=True, stop=True).then_inc(done, 1)
                filler(1, 7)
                warm(2)

                for c in pr.chs:
                    pe.wait_ge(V, pr.at("V", "bv"))
                    if c == 1:
                        pe.wait_ge(A, pr.at("A", "at"))
                    settled(pe)
                    for j in range(4):
                        for par in range(2):
                            r, x_ = half_rows(par), j * n + c
                            l = bkk[r, x_].rearrange("p a w -> p (a w)")
                            m = ra[r, x_, :, :].rearrange("p a w -> p (a w)")
                            mm = pe.matmul(PS[:, 4 + 2 * c + par, 128 * j:128 * j + 128], l, m, start=True, stop=True)
                    step(f"lm{c}")
                    mm.then_inc(done, 1)

                def tiles(bank, col, lhs, rhs, turn=False):
                    for j in range(4):
                        for par in range(2):
                            src = half_rows(1 - par if turn else par)
                            mm = pe.matmul(PS[half_rows(par), bank, col + CH * j:col + CH * j + CH],
                                           lhs(src, j, par), rhs(src, j, par), start=True, stop=True)
                    return mm

                def of(t):
                    return lambda r, j, par: t[r, j, :]

                def part(t, k):
                    return lambda r, j, par: t[r, k, j, :]

                for c in pr.chs:
                    b0_, b1_ = 4 + 2 * c, 5 + 2 * c
                    warm()
                    pe.wait_ge(V, pr.at("V", f"ydO{c}"))
                    settled(pe)
                    tiles(b0_, 0, lambda r, j, par: ra[r, j * n + c, 1, :], lambda r, j, par: bkk[r, j * n + c, par, :])
                    for j in range(4):
                        for par in range(2):
                            mm = pe.matmul(PS[half_rows(1 - par), b0_, 256 + CH * j:256 + CH * j + CH],
                                           xsl(8 + j, CH * c, CH * c + CH), mat[:, M_ID, half_rows(par)],
                                           start=True, stop=True)
                    step(f"xv{c}")
                    mm.then_inc(done, 1)
                    for j in range(4):
                        l = bkk[:, j * n + c].rearrange("p a w -> p (a w)")
                        mm = pe.transpose(PS[:, b1_, 128 * j:128 * j + 128], l, mat[:, M_ID])
                    step(f"tok{c}")
                    mm.then_inc(done, 1)

                for c in pr.chs:
                    warm()
                    pe.wait_ge(V, pr.at("V", f"xd{c}"))
                    pe.wait_ge(A, pr.at("A", f"tok{c}"))
                    settled(pe)
                    tiles(5 + 2 * c, 0, of(yd[c]), of(xd[c]))
                    step(f"s1_{c}")
                    tiles(5 + 2 * c, 256, of(xd[c]), of(yd[c])).then_inc(done, 1)
                for c in pr.chs:
                    warm()
                    pe.wait_ge(V, pr.at("V", f"svO{c}"))
                    pe.wait_ge(A, pr.at("A", f"xy2{c}"))
                    pe.wait_ge(G, pr.at("G", f"pt1{c}"))
                    settled(pe)
                    tiles(4 + 2 * c, 0, part(xy[c], 1), part(xy[c], 0))
                    tiles(4 + 2 * c, 256, part(xy[c], 0), part(xy[c], 1))
                    step(f"s2_{c}")
                    tiles(5 + 2 * c, 0, part(xy[c], 0), of(pt[c])).then_inc(done, 1)
                for c in pr.chs:
                    warm()
                    pe.wait_ge(V, pr.at("V", f"pt2{c}"))
                    pe.wait_ge(A, pr.at("A", f"xy4{c}"))
                    settled(pe)
                    tiles(4 + 2 * c, 0, part(xy4[c], 1), part(xy4[c], 0))
                    step(f"s3_{c}")
                    tiles(5 + 2 * c, 0, part(xy4[c], 0), of(pt[c])).then_inc(done, 1)
                for c in pr.chs:
                    warm()
                    pe.wait_ge(V, pr.at("V", f"pt3{c}"))
                    pe.wait_ge(A, pr.at("A", f"x8{c}"))
                    settled(pe)
                    step(f"s4_{c}")
                    tiles(4 + 2 * c, 0, of(xd[c]), of(pt[c])).then_inc(done, 1)
                for c in pr.chs:
                    warm()
                    pe.wait_ge(V, pr.at("V", f"dt{c}"))
                    settled(pe)
                    step(f"s5_{c}")
                    tiles(5 + 2 * c, 0, of(pt[c]), lambda r, j, par: mat[r, M_ID, r]).then_inc(done, 1)
                    step(f"lv{c}")
                    tiles(4 + 2 * c, 0, lambda r, j, par: lm[c][r, par, j, CH:128],
                          lambda r, j, par: sv[c][r, j, par, :], turn=True).then_inc(done, 1)
                for c in pr.chs:
                    warm()
                    pe.wait_ge(A, pr.at("A", f"d{c}"))
                    pe.wait_ge(G, pr.at("G", f"pt1{c}"))
                    settled(pe)
                    tiles(5 + 2 * c, 0, of(yd[c]), of(yo[c]))
                    step(f"s6_{c}")
                    tiles(5 + 2 * c, 256, of(yo[c]), of(yd[c])).then_inc(done, 1)
                for c in pr.chs:
                    warm()
                    pe.wait_ge(A, pr.at("A", f"g{c}"))
                    settled(pe)
                    tiles(4 + 2 * c, 0, part(xy[c], 0), part(xy[c], 1))
                    step(f"s7_{c}")
                    tiles(5 + 2 * c, 0, part(xy[c], 1), of(pt[c])).then_inc(done, 1)
                for c in pr.chs:
                    warm()
                    pe.wait_ge(V, pr.at("V", f"rr{c}"))
                    pe.wait_ge(A, pr.at("A", f"h{c}"))
                    settled(pe)
                    step(f"s8_{c}")
                    tiles(4 + 2 * c, 0, of(xd[c]), of(pt[c])).then_inc(done, 1)
                for c in pr.chs:
                    b0_, b1_ = 4 + 2 * c, 5 + 2 * c
                    if c:
                        pe.wait_ge(V, pr.at("V", "st20"))
                    elif not pr.sample:
                        pe.wait_ge(s_reset, 2)
                    pe.wait_ge(V, pr.at("V", f"tt{c}"))
                    settled(pe)
                    step(f"q0{c}")
                    tiles(b1_, 0, lambda r, j, par: ra[r, j * n + c, 1, :], of(st)).then_inc(done, 1)
                    step(f"o1{c}")
                    tiles(b0_, 0, of(st), lambda r, j, par: ra[r, j * n + c, 0, :]).then_inc(done, 1)
                    warm()
                    pe.wait_ge(V, pr.at("V", f"x{c}"))
                    settled(pe)
                    step(f"sa{c}")
                    tiles(b1_, 0, of(pt[c]), of(yo[c])).then_inc(done, 1)
                    warm()
                    pe.wait_ge(V, pr.at("V", f"saO{c}"))
                    settled(pe)
                    for j in range(4):
                        for par in range(2):
                            mm = pe.matmul(PS[half_rows(par), b1_, CH * j:CH * j + CH], tk[c][:, j, par, :],
                                           sv[c][:, j, par, :], start=True, stop=True)
                    step(f"ds{c}")
                    mm.then_inc(done, 1)
                    warm()
                    pe.wait_ge(A, pr.at("A", f"o1{c}"))
                    settled(pe)
                    for j in range(4):
                        for par in range(2):
                            mm = pe.matmul(PS[half_rows(par), b0_, CH * j:CH * j + CH], sv[c][:, j, par, :],
                                           lm[c][:, par, j, 0:CH], start=True, stop=True)
                    step(f"o2{c}")
                    mm.then_inc(done, 1)
                warm()
                pe.wait_ge(V, pr.at("V", f"o{pr.chs[-1]}"))
                settled(pe)
                step("mean")
                pe.matmul(PS[:, 4, 0:4 * W], mat[:, M_MEAN], flat(ip), start=True, stop=True).then_inc(done, 1)
                warm()
                pe.wait_ge(A, pr.at("A", "osq"))
                settled(pe)
                step("var")
                pe.matmul(PS[:, 5, 0:4 * W], mat[:, M_MEAN], flat(aa), start=True, stop=True).then_inc(done, 1)
                step.end()

            def body(pe, b, b0):
                with pe.Fori(0, NPL // 2) as i:
                    for p in range(2):
                        wk = (lambda k: (n1_lo, b * KD + (k + 1))) if p == 0 else None
                        unit(b, b0, p, i, hh, hl, 2 * p, 2, wait_k=wk).then_inc(mm_done, 1)
                if b0:
                    pair_steps(b, b0, Pair(None, 0), None)
                with pe.Fori(0, NPAIR) as i:
                    pair_steps(b, b0, Pair(b * NPAIR + i, i * 128 + (CH if b0 else 0)), i)
                for e in "AV":
                    pe.wait_ge(rw[e], Pair(b * NPAIR + (NPAIR - 1), 0).all(e))
                settled(pe)
                with pe.Fori(0, KD) as d:
                    unit(b, b0, U_BR, d, hh, hl, 2, 2).then_inc(mm_done, 1)
                    unit(b, b0, U_BR + 1, d, ath, atl, 4, 2, range(4),
                         wait_k=lambda k: (b_lo, b * 8 + (k + 1)))
                    unit(b, b0, U_BR + 1, d, rwh, rwl, 6, 2, range(4, 8), 4,
                         wait_k=lambda k: (b_lo, b * 8 + (k + 1))).then_inc(mm_done, 1)
                with pe.Fori(0, KD // 2) as i:
                    for p in range(2):
                        unit(b, b0, U_WO + p, i, mh, ml, 2 * p, 2,
                             wait_k=lambda k: (m_lo, b * KD + (k + 2))).then_inc(mm_done, 1)
                pe.wait_ge(n2_sum, summed(b * 2, KD))
                settled(pe)
                norm_sum(b0, acc, 4).then_inc(n2_ms, 1)
                for s, g in enumerate(GROUPS):
                    with pe.Fori(0, g) as i:
                        for p in range(2):
                            wk = (lambda k: (n2_lo, b * KD + (k + 1))) if p == 0 and s == 0 else None
                            unit(b, b0, U_F[s] + p, i, hh, hl, 2 * p, 2, wait_k=wk).then_inc(mm_done, 1)
                    pe.wait_ge(f_lo, b * NFF + (sum(GROUPS[:s + 1]) + 1))
                    settled(pe)
                    with pe.Fori(0, KD // 2) as i:
                        for p in range(2):
                            unit(b, b0, U_F[s] + 2 * g + p, i, fh, fl, 2 * p, 2, range(g)).then_inc(mm_done, 1)
                    if s == 1:
                        pe.wait_ge(n1_sum, b * (KD + 1) + 2 * (KD + 1))
                        settled(pe)
                        norm_sum(False, nsum, 4).then_inc(n1_ms, 1)
                pe.wait_ge(n2_sum, summed(b * 2 + 1, KD))
                settled(pe)
                norm_sum(b0, acc, 6).then_inc(n2_ms, 1)

            pe.wait_ge(ld, LDALL)
            pe.wait_ge(n1_sum, KD + 1)
            norm_sum(True, nsum, 4).then_inc(n1_ms, 1)
            pe.matmul(PS[:, 6, 0:2], mat[:, M_ONE], mat[:, M_ONE, 0:2], start=True, stop=True).then_inc(mm_done, 2)
            blocks(pe, body)

        @block.scalar
        def _(act):
            def split(b, off, i, first=False):
                u, p = ring(b, off, i), off % 2
                act.wait_ge(w_ld[p], landed(b, off, i))
                if not isinstance(u, int) or u >= 2:
                    act.wait_ge(mm_done, mmd(u - 2) if isinstance(u, int) else u + 1)
                act.activation(wh[p][:], raw[p][:], ACT.Copy).then_inc(hi_done, 1)

            def squares(T, src, out, sem_sq, sem_sum, count):
                if not isinstance(count, int) or count > 0:
                    act.wait_ge(sem_sum, count)
                settled(act)
                act.activation(out[:, 0:T], src, ACT.Square).then_inc(sem_sq, 1)

            def log_exp():
                act.preload_act_table_set("natural_log_exp_and_others")

            def rstd(T, b0, bank, out, sem_ms, ms, sem_rs, rsn):
                act.wait_ge(sem_ms, ms)
                act.activation(view(out[:, 0:T], b0), psv(bank, b0), ACT.Ln, bias=bias[:, 0:1],
                               scale=1.0 / D).then_inc(sem_rs, 1)
                act.wait_ge(sem_rs, rsn + 1)
                act.activation(out[:, 0:T], out[:, 0:T], ACT.Exp, scale=-0.5).then_inc(sem_rs, 1)

            def pair_steps(b, b0, pr, i):
                step = Order(pr, "A")
                V, A, G, Tn = rw["V"], rw["A"], rw["G"], rw["T"]
                W, n = pr.w, pr.n

                def v4(t):
                    return t[:].rearrange("p a w -> p (a w)")[:, 0:4 * W]

                xsf = xs[:].rearrange("p a w -> p (a w)")

                def go(name, out, in_, func, **kw):
                    step(name)
                    act.activation(out, in_, func, **kw).then_inc(A, 1)

                def gates_in(f):
                    act.wait_ge(mm_done, mmd(ring(b, U_GA + f, i)))
                    settled(act)
                    act.activation(view(ga[:, i * 2 + f, 0:T_(b0)], b0), psv(0, b0), ACT.Copy).then_inc(bank_free, 1)

                act.preload_act_table_set("sigmoid_and_others")
                act.wait_ge(G, pr.at("G", "xs3"))
                go("et", xsf[0:64, 12 * W:13 * W], xsf[0:64, 12 * W:13 * W], ACT.Tanh)
                go("eg", xsf[:, 13 * W:14 * W], xsf[:, 13 * W:14 * W], ACT.Sigmoid)
                act.wait_ge(G, pr.at("G", "kk"))
                go("ksq", v4(pp), v4(kk), ACT.Square)
                if not pr.sample:
                    split(b, U_GA + 1, i)
                act.wait_ge(Tn, pr.at("T", "vt"))
                go("vt", vtk[:].rearrange("p c w -> p (c w)")[:, 0:128 * n], PS[:, 6, 0:128 * n], ACT.Copy)
                act.wait_ge(V, pr.at("V", "z1"))
                go("z2", v4(zz), v4(zz), ACT.Sigmoid)
                act.wait_ge(V, pr.at("V", "a1"))
                go("a2", v4(aa), v4(aa), ACT.Sigmoid)
                log_exp()
                act.wait_ge(V, pr.at("V", "sub"))
                go("ex", sm[:, 0:n], sm[:, 0:n], ACT.Exp)
                act.wait_ge(V, pr.at("V", "sk"))
                go("es", mxs[:, 1, 0:4 * n], mxs[:, 1, 0:4 * n], ACT.Exp)
                act.wait_ge(Tn, pr.at("T", "g"))
                go("gcp", v4(gg), PS[:, 6, 0:4 * W], ACT.Copy)
                if not pr.sample:
                    gates_in(0)
                act.wait_ge(V, pr.at("V", "n1"))
                go("n2", v4(pp), v4(pp), ACT.Ln, scale=2.0 ** 20)
                act.wait_ge(A, pr.at("A", "n2"))
                go("n3", v4(pp), v4(pp), ACT.Exp, scale=-0.5, bias=bias[:, 2:3])
                act.wait_ge(G, pr.at("G", "cm"))
                go("pm", v4(zz), v4(zz), ACT.Exp, scale=-EXPM05)
                act.wait_ge(G, pr.at("G", "kkn"))
                go("p", v4(pp), v4(cc), ACT.Exp, scale=-EXPM05)
                go("ip", v4(ip), v4(cc), ACT.Exp, scale=EXPM05)
                act.wait_ge(Tn, pr.at("T", "ptr"))
                go("ptr", ptk[:, 0:n].rearrange("p c a w -> p (c a) w"),
                   PS[:, 2:2 + n, :].rearrange("p c (a w) -> p (c a) w", a=4), ACT.Copy)
                act.wait_ge(Tn, pr.at("T", "pv"))
                settled(act)
                step("at")
                qv = q[:, :, 0:CH] if pr.sample else q[:, :, bass.ds(pr.tok, 128)]
                act.activation(qv.rearrange("p a (c w) -> p a c w", c=n),
                               PS[:, 7, 0:256 * n].rearrange("p (c a w) -> p a c w", c=n, a=4), ACT.Copy).then_inc(A, 1)
                if not pr.sample:
                    split(b, U_GA + 2, i)
                    gates_in(1)

                def flat2(t):
                    return t[:].rearrange("p k a w -> p (k a w)")

                def fl(t):
                    return t[:].rearrange("p a w -> p (a w)")

                def copies(name, st_, out, bank, width):
                    for c in pr.chs:
                        act.wait_ge(Tn, pr.at("T", f"{st_}{c}"))
                        go(f"{name}{c}", out(c), PS[:, bank + 2 * c, 0:width], ACT.Copy)

                copies("tok", "tok", lambda c: tk[c][:].rearrange("p a k w -> p (a k w)"), 5, 512)
                copies("xy2", "s1_", lambda c: flat2(xy[c]), 5, 512)
                copies("xy4", "s2_", lambda c: flat2(xy4[c]), 4, 512)
                copies("x8", "s3_", lambda c: fl(xd[c]), 4, 256)
                copies("d", "s5_", lambda c: fl(yd[c]), 5, 256)
                copies("zl", "lv", lambda c: fl(zl[c]), 4, 256)
                copies("g", "s6_", lambda c: flat2(xy[c]), 5, 512)
                copies("h", "s7_", lambda c: fl(xd[c]), 4, 256)
                for c in pr.chs:
                    act.wait_ge(Tn, pr.at("T", f"o1{c}"))
                    go(f"o1{c}", v4(ip).rearrange("p (a w) -> p a w", a=4)[:, :, CH * c:CH * c + CH],
                       PS[:, 4 + 2 * c, 0:256].rearrange("p (a w) -> p a w", a=4), ACT.Copy)
                act.wait_ge(V, pr.at("V", "oc"))
                go("osq", v4(aa), v4(ip), ACT.Square)
                act.wait_ge(Tn, pr.at("T", "var"))
                go("v1", v4(zz), PS[:, 5, 0:4 * W], ACT.Ln, bias=bias[:, 1:2])
                act.wait_ge(A, pr.at("A", "v1"))
                go("v2", v4(zz), v4(zz), ACT.Exp, scale=-0.5)
                step.end()

            def body(act, b, b0):
                T = T_(b0)
                log_exp()
                with act.Fori(0, NPL // 2) as i:
                    split(b, 1, i)
                    split(b, 2, i)
                if b0:
                    pair_steps(b, b0, Pair(None, 0), None)
                with act.Fori(0, NPAIR) as i:
                    pair_steps(b, b0, Pair(b * NPAIR + i, i * 128 + (CH if b0 else 0)), i)
                last = Pair(b * NPAIR + (NPAIR - 1), 0)
                act.wait_ge(rw["G"], last.all("G"))
                act.wait_ge(rw["V"], last.all("V"))
                act.wait_ge(rw["T"], last.all("T"))
                act.wait_ge(rw["A"], last.all("A"))
                for j in range(8):
                    dst, src = (ath, q) if j < 4 else (rwh, rwp)
                    act.activation(dst[:, j % 4, 0:T], src[:, j % 4, 0:T], ACT.Copy).then_inc(b_hi, 1)
                act.preload_act_table_set("sigmoid_and_others")
                with act.Fori(0, KD) as d:
                    split(b, U_BR + 1, d)
                    act.wait_ge(mm_done, mmd(ring(b, U_BR, d)))
                    act.wait_ge(m_sum, b * KD + d + 1)
                    if b0:
                        act.wait_ge(b_lo, 8)
                    else:
                        act.wait_ge(b_lo, b * 8 + 8)
                    act.activation(view(e1[:, 0:T], b0), psv(2, b0), ACT.Sigmoid).then_inc(bank_free, 1)
                    act.activation(e2[:, 0:T], ga[:, d, 0:T], ACT.Sigmoid).then_inc(gates, 1)
                    split(b, U_BR + 2, d)
                    act.wait_ge(m_sum, b * KD + d + 2)
                    settled(act)
                    act.activation(mh[:, d, 0:T], acc[:, 0:T], ACT.Copy).then_inc(m_hi, 1)
                log_exp()
                with act.Fori(0, KD // 2) as i:
                    for p in range(2):
                        split(b, U_WO + p + 1, i)
                        act.wait_ge(bank_free, free(ring(b, U_WO + p, i)))
                        squares(T, xres[:, i * 2 + p, 0:T], sq[p], n2_sq, n2_sum, summed(b * 2, i * 2 + (p - 1)))
                if not b0:
                    act.wait_ge(y_done, b * KD)
                rstd(T, b0, 4, rs, n2_ms, b * 2 + 1, n2_rs, b * 4)
                for d in range(KD):
                    act.wait_ge(n2_t, b * KD + (d + 1))
                    act.activation(hh[:, d, 0:T], sq[d % 2][:, 0:T], ACT.Copy).then_inc(n2_hi, 1)
                for s, g in enumerate(GROUPS):
                    before = sum(GROUPS[:s])
                    act.preload_act_table_set("silu_and_others")
                    with act.Fori(0, g) as i:
                        split(b, U_F[s] + 1, i)
                        f = b * NFF + i + before
                        act.wait_ge(mm_done, mmd(ring(b, U_F[s], i)))
                        act.wait_ge(bank_free, free(ring(b, U_F[s] - 1, i)))
                        act.activation(view(e1[:, 0:T], b0), psv(0, b0), ACT.Silu).then_inc(bank_free, 1)
                        split(b, U_F[s] + 2, i)
                        act.wait_ge(bank_free, free(ring(b, U_F[s] + 1, i)))
                        settled(act)
                        act.activation(fh[:, i, 0:T], acc[:, 0:T], ACT.Copy).then_inc(f_hi, 1)
                    if s:
                        log_exp()
                    with act.Fori(0, KD // 2) as i:
                        for p in range(2):
                            off = U_F[s] + 2 * g + p
                            split(b, off + 1, i)
                            if s == 1:
                                act.wait_ge(xin_ld, b * 16 + 32)
                                squares(BT, xin[:, i * 2 + p, 0:BT], nt[p], n1_sq, n1_sum,
                                        b * (KD + 1) + i * 2 + (p + KD + 1))
                            if s == 2:
                                act.wait_ge(n1_t, b * KD + i * 2 + (p + KD + 1))
                                settled(act)
                                act.activation(hh[:, i * 2 + p, 0:BT], nt[p][:, 0:BT], ACT.Copy).then_inc(n1_hi, 1)
                                act.wait_ge(bank_free, free(ring(b, off, i)))
                                squares(T, xres[:, i * 2 + p, 0:T], sq[p], n2_sq, n2_sum,
                                        summed(b * 2 + 1, i * 2 + (p - 1)))
                    if s == 1:
                        rstd(BT, False, 4, nrs, n1_ms, b + 2, n1_rs, b * 2 + 2)
                rstd(T, b0, 6, rs, n2_ms, b * 2 + 2, n2_rs, b * 4 + 2)
                for d in range(KD):
                    act.wait_ge(y_done, b * KD + (d + 1))
                    settled(act)
                    dst = y[:, d, 0:MT] if b0 else y[:, d, bass.ds(b * BT + CH, BT)]
                    act.dma_start(dst, xres[:, d, 0:T]).then_inc(y_st, 16)

            log_exp()
            act.wait_ge(ld, LDALL)
            act.wait_ge(ini, 3)
            for d in range(KD):
                act.wait_ge(xin_ld, 16)
                squares(MT, xin[:, d, :], nt[d % 2], n1_sq, n1_sum, d)
            rstd(MT, True, 4, nrs, n1_ms, 1, n1_rs, 0)
            split(0, 0, 0)
            for d in range(KD):
                act.wait_ge(n1_t, d + 1)
                act.activation(hh[:, d, :], nt[d % 2][:], ACT.Copy).then_inc(n1_hi, 1)
            blocks(act, body)

        @block.gpsimd
        def _(pool):
            def pair_steps(b, b0, pr, i):
                step = Order(pr, "G")
                V, A, G, Tn = rw["V"], rw["A"], rw["G"], rw["T"]
                W, n = pr.w, pr.n

                def own(name):
                    pool.wait_ge(G, pr.at("G", name))
                    settled(pool)

                def v4(t):
                    return t[:].rearrange("p a w -> p (a w)")[:, 0:4 * W].rearrange("p (a w) -> p a w", a=4)

                xsv = xs[:].rearrange("p a w -> p (a w)")[:, 0:NRW * W].rearrange("p (a w) -> p a w", a=NRW)

                def tt_(name, out, a, bb_, op):
                    step(name)
                    pool.tensor_tensor(out, a, bb_, op).then_inc(G, 1)

                def cols(t, off, width):
                    return t[:, :, off:off + width] if pr.sample else t[:, :, bass.ds(pr.tok + off, width)]

                if not pr.sample:
                    pool.wait_ge(Tn, pr.base["T"] - back("T", "tok0"))
                settled(pool)
                tt_("xs1", xsv, cols(rwp, 0, W), cols(rwp, 1, W), ALU.subtract)
                own("xs1")
                tt_("xs2", xsv, xsv, cv(C_MU, NRW, W), ALU.mult)
                own("xs2")
                tt_("xs3", xsv, xsv, cols(rwp, 1, W), ALU.add)
                own("xs3")
                tt_("kk", v4(kk), xsv[:, 4:8], cv(C_KK, 4, W), ALU.mult)
                if not pr.sample:
                    pool.wait_ge(Tn, pr.base["T"] - back("T", "s4_0"))
                pool.wait_ge(bank_free, b * NU + free(NPL - 1))
                settled(pool)
                step("qb")
                pool.tensor_copy(qb[:, :, 0:W], cols(q, 0, W)).then_inc(G, 1)
                step("kvb")
                pool.tensor_copy(kvb[:, :, 0:CH + W], cols(kvp, 0, CH + W)).then_inc(G, 1)
                pool.wait_ge(V, pr.at("V", "scan"))
                settled(pool)
                tt_("cm", v4(zz), v4(cc), v4(zz), ALU.subtract)
                pool.wait_ge(A, pr.at("A", "n3"))
                settled(pool)
                tt_("kkn", v4(kk), v4(kk), v4(pp), ALU.mult)
                pool.wait_ge(A, pr.at("A", "ip"))
                tt_("bo1", v4(cc), xsv[:, 0:4], cv(C_RK, 4, W), ALU.mult)
                own("bo1")
                pool.wait_ge(V, pr.at("V", "ktm" if pr.sample else "kt2"))
                settled(pool)
                tt_("bo2", v4(cc), v4(cc), v4(kt), ALU.mult)
                for c in pr.chs:
                    for par, name in enumerate(("E", "O")):
                        r = half_rows(par)
                        own(("bo2" if c == 0 else "pt10") if par == 0 else f"yoE{c}")
                        pool.wait_ge(V, pr.at("V", f"lm{name}{c}"))
                        settled(pool)
                        tt_(f"yo{name}{c}", yo[c][r], lm[c][r, par, :, CH:128], mrep(M_YD, 4, 64 * par, 64 * par + 64, 64, 128),
                            ALU.mult)
                    pool.wait_ge(V, pr.at("V", f"ydO{c}"))
                    own(f"yoO{c}")
                    tt_(f"pt1{c}", pt[c][:], yd[c][:], mrep(M_XD, 4, c0=64, c1=128), ALU.add)
                pool.wait_ge(V, pr.at("V", "bv"))
                own(f"pt1{pr.chs[-1]}")
                tt_("lb", v4(kt), v4(kt), cv(C_LB, 4, W), ALU.add)
                step.end()

            def body(pool, b, b0):
                T = T_(b0)
                pool.wait_ge(bank_free, b * NU + free(NRW - 1))
                if b0:
                    pool.tensor_copy(rwp[:, :, 0:1], rws[:]).then_inc(shift_sv, 1)
                    pool.wait_ge(shift_sv, 1)
                    pool.tensor_copy(rws[:], rwp[:, :, NSAMP:NSAMP + 1]).then_inc(shift_sv, 1)
                    pair_steps(b, b0, Pair(None, 0), None)
                    pool.wait_ge(s_shift, 16)
                else:
                    pool.wait_ge(y_st, b * (16 * KD))
                    pool.wait_ge(saved, b * 2)
                    settled(pool)
                    pool.tensor_copy(kvp[:, :, 0:CH], kvs[:, :, CH:2 * CH]).then_inc(lead, 1)
                    pool.tensor_copy(rwp[:, :, 0:1], rws[:]).then_inc(lead, 1)
                    pool.wait_ge(lead, b * 2)
                    settled(pool)
                with pool.Fori(0, NPAIR) as i:
                    pair_steps(b, b0, Pair(b * NPAIR + i, i * 128 + (CH if b0 else 0)), i)
                pool.tensor_copy(kvs[:], kvp[:, :, CH + T - 128:CH + T]).then_inc(saved, 1)
                pool.tensor_copy(rws[:], rwp[:, :, T:T + 1]).then_inc(saved, 1)
                for j in range(8):
                    dst, hi, src = (atl, ath, q) if j < 4 else (rwl, rwh, rwp)
                    pool.wait_ge(b_hi, b * 8 + (j + 1))
                    settled(pool)
                    pool.tensor_tensor(dst[:, j % 4, 0:T], src[:, j % 4, 0:T], hi[:, j % 4, 0:T],
                                       ALU.subtract).then_inc(b_lo, 1)
                with pool.Fori(0, KD) as d:
                    pool.wait_ge(m_hi, b * KD + d + 1)
                    settled(pool)
                    pool.tensor_tensor(ml[:, d, 0:T], acc[:, 0:T], mh[:, d, 0:T], ALU.subtract).then_inc(m_lo, 1)
                for d in range(KD):
                    pool.wait_ge(n2_hi, b * KD + (d + 1))
                    settled(pool)
                    pool.tensor_tensor(hl[:, d, 0:T], sq[d % 2][:, 0:T], hh[:, d, 0:T],
                                       ALU.subtract).then_inc(n2_lo, 1)
                for s, g in enumerate(GROUPS):
                    with pool.Fori(0, g) as i:
                        pool.wait_ge(f_hi, b * NFF + i + (sum(GROUPS[:s]) + 1))
                        settled(pool)
                        pool.tensor_tensor(fl[:, i, 0:T], acc[:, 0:T], fh[:, i, 0:T], ALU.subtract).then_inc(f_lo, 1)
                with pool.Fori(0, KD // 2) as i:
                    for p in range(2):
                        pool.wait_ge(n1_hi, b * KD + i * 2 + (p + KD + 1))
                        settled(pool)
                        pool.tensor_tensor(hl[:, i * 2 + p, 0:BT], nt[p][:, 0:BT], hh[:, i * 2 + p, 0:BT],
                                           ALU.subtract).then_inc(n1_lo, 1)

            pool.wait_ge(ld, LDALL)
            pool.memset(scratch[:, 0:1], 0.0).then_inc(m_lo, 1)
            pool.memset(scratch[:, 1:2], 0.0).then_inc(f_lo, 1)
            for d in range(KD):
                pool.wait_ge(n1_hi, d + 1)
                pool.tensor_tensor(hl[:, d, :], nt[d % 2][:], hh[:, d, :], ALU.subtract).then_inc(n1_lo, 1)
            blocks(pool, body)

        @block.vector
        def _(dve):
            def split(b, off, i):
                u, p = ring(b, off, i), off % 2
                dve.wait_ge(hi_done, u + 1)
                dve.tensor_tensor(wl[p][:], raw[p][:], wh[p][:], ALU.subtract).then_inc(lo_done, 1)

            def clear(s, sem_sum, wait):
                dve.wait_ge(*wait)
                dve.memset(s[:], 0.0).then_inc(sem_sum, 1)

            def add_sq(T, s, src, sem_sq, nth, sem_sum, count):
                dve.wait_ge(sem_sq, nth)
                dve.wait_ge(sem_sum, count)
                dve.tensor_tensor(s[:, 0:T], s[:, 0:T], src[:, 0:T], ALU.add).then_inc(sem_sum, 1)

            def scaled(T, out, src, c, d, r):
                return dve.scalar_tensor_tensor(out=out, in0=src, scalar=cst[:, c + d:c + d + 1],
                                                in1=r[:, 0:T], op0=ALU.mult, op1=ALU.mult)

            def pair_steps(b, b0, pr, i):
                step = Order(pr, "V")
                V, A, G, Tn = rw["V"], rw["A"], rw["G"], rw["T"]
                W, n = pr.w, pr.n

                def own(name):
                    dve.wait_ge(V, pr.at("V", name))

                def v4(t):
                    return t[:].rearrange("p a w -> p (a w)")[:, 0:4 * W].rearrange("p (a w) -> p a w", a=4)

                def v8(t):
                    return t[:].rearrange("p a w -> p (a w)")[:, 0:4 * W].rearrange("p (a w) -> p a w", w=CH)

                def fl(t):
                    return t[:].rearrange("p a w -> p (a w)")[:, 0:4 * W]

                xsf = xs[:].rearrange("p a w -> p (a w)")

                def xp(plane):
                    return xsf[:, plane * W:(plane + 4) * W]

                def ps(bank):
                    return PS[:, bank, 0:4 * W]

                def tt_(name, out, a, bb_, op):
                    step(name)
                    dve.tensor_tensor(out, a, bb_, op).then_inc(V, 1)

                def ts_(name, out, a, s1, s2, op0, op1=None):
                    step(name)
                    (dve.tensor_scalar(out, a, s1, s2, op0, op1) if op1 else
                     dve.tensor_scalar(out, a, s1, None, op0)).then_inc(V, 1)

                def rc_(name, out, a):
                    step(name)
                    dve.reciprocal(out, a).then_inc(V, 1)

                def stt_(name, out, a, s, bb_, op0, op1):
                    step(name)
                    dve.scalar_tensor_tensor(out=out, in0=a, scalar=s, in1=bb_, op0=op0, op1=op1).then_inc(V, 1)

                def q4(bank, width):
                    return PS[:, bank, 0:4 * width].rearrange("p (a w) -> p a w", a=4)

                def heads(t):
                    return t.rearrange("p c a w -> p (c a) w")

                m0, m1, m2 = (mxs[:, k, 0:4 * n] for k in range(3))
                sink = cst[:, C_SINK:C_SINK + 4].unsqueeze(1).to_broadcast([128, n, 4])
                smn = sm[:, 0:n]
                if not pr.sample:
                    split(b, U_GA + 1, i)
                dve.wait_ge(Tn, pr.at("T", "s"))
                if not pr.sample:
                    dve.wait_ge(s_reset, 2)
                    dve.wait_ge(V, pr.base["V"])
                for c in pr.chs:
                    stt_(f"sm{c}", sm[:, c], q4(2 + c, 128), SCALE,
                         kmask[:, c, :].unsqueeze(1).to_broadcast([128, 4, 128]), ALU.mult, ALU.add)
                own(f"sm{pr.chs[-1]}")
                step("mx")
                dve.tensor_reduce(m0, heads(smn), AX, ALU.max).then_inc(V, 1)
                own("mx")
                c4 = (lambda t: t.rearrange("p (c a) -> p c a", a=4))
                tt_("mx2", c4(m0), c4(m0), sink, ALU.max)
                own("mx2")
                tt_("sub", heads(smn), heads(smn), m0.unsqueeze(2).to_broadcast([128, 4 * n, 128]), ALU.subtract)
                tt_("sk", c4(m1), sink, c4(m0), ALU.subtract)
                dve.wait_ge(Tn, pr.at("T", "z"))
                tt_("z1", v4(zz), q4(4, W), cv(C_W0, 4, W), ALU.add)
                dve.wait_ge(Tn, pr.at("T", "a"))
                tt_("a1", v4(aa), q4(5, W), cv(C_A0, 4, W), ALU.add)
                dve.wait_ge(Tn, pr.at("T", "kn"))
                ts_("n1", fl(pp), ps(7), 1e-24, None, ALU.max)
                dve.wait_ge(A, pr.at("A", "z2"))
                vm = vmask[:].unsqueeze(1).to_broadcast([128, 4, CH])
                if pr.sample:
                    tt_("lwm", v4(zz), v4(zz), vm, ALU.mult)
                    own("lwm")
                step("scan")
                dve.tensor_tensor_scan(fl(cc), scanm[:].rearrange("p a w -> p (a w)")[:, 0:4 * W], fl(zz), 0.0,
                                       ALU.mult, ALU.add).then_inc(V, 1)
                dve.wait_ge(A, pr.at("A", "a2"))
                stt_("kt1", v4(kt), v4(aa), -1.0, cv(C_KA, 4, W), ALU.add, ALU.mult)
                own("kt1")
                stt_("kt2", fl(kt), fl(kt), 1.0, xp(4), ALU.add, ALU.mult)
                if pr.sample:
                    own("kt2")
                    tt_("ktm", v4(kt), v4(kt), vm, ALU.mult)
                dve.wait_ge(A, pr.at("A", "es"))
                step("sum")
                dve.tensor_reduce(m2, heads(smn), AX, ALU.add).then_inc(V, 1)
                own("sum")
                tt_("den", m2, m2, m1, ALU.add)
                own("den")
                rc_("rec", m2, m2)
                own("rec")
                tt_("pn", heads(smn), heads(smn), m2.unsqueeze(2).to_broadcast([128, 4 * n, 128]), ALU.mult)
                dve.wait_ge(G, pr.at("G", "kkn"))
                tt_("bb", fl(aa), fl(kk), fl(aa), ALU.mult)
                if pr.sample:
                    own("bb")
                    tt_("bbm", v4(aa), v4(aa), vm, ALU.mult)
                dve.wait_ge(A, pr.at("A", "ip"))
                own("bbm" if pr.sample else "bb")
                stt_("at", ra[:, 0:4 * n, 1, :], v8(kk), -1.0, v8(zz), ALU.mult, ALU.mult)
                tt_("rt", ra[:, 0:4 * n, 0, :], xp(0).rearrange("p (a w) -> p a w", w=CH), v8(pp), ALU.mult)
                step("pc")
                dve.tensor_copy(pcf[:, 0:4 * n], v8(pp)[:, :, CH - 1]).then_inc(V, 1)
                for name, t, first in (("bt", aa, 0), ("kt", kt, 1)):
                    for par in range(2):
                        r = half_rows(par)
                        tt_(name + "EO"[par], bkk[r, 0:4 * n, first ^ par, :], v8(t)[r], v8(ip)[r], ALU.mult)
                dve.wait_ge(Tn, pr.at("T", "bo"))
                own("ktO")
                tt_("bv", fl(kt), ps(4), xp(8), ALU.mult)
                if not pr.sample:
                    split(b, U_GA + 2, i)

                def q8(bank, r=slice(0, 128), c0=0, width=CH):
                    return PS[r, bank, c0:c0 + 4 * width].rearrange("p (a w) -> p a w", a=4)

                for c in pr.chs:
                    dve.wait_ge(Tn, pr.at("T", f"lm{c}"))
                    for par, name in enumerate(("E", "O")):
                        tt_(f"lm{name}{c}", lm[c][:, par], q4(4 + 2 * c + par, 128), mrep(M_LM, 4), ALU.mult)
                    for par, name in enumerate(("E", "O")):
                        r = half_rows(par)
                        tt_(f"yd{name}{c}", yd[c][r], q4(4 + 2 * c + par, 128)[r, :, CH:128],
                            mrep(M_YD, 4, 64 * par, 64 * par + 64, 0, 64), ALU.mult)
                for c in pr.chs:
                    dve.wait_ge(Tn, pr.at("T", f"xv{c}"))
                    tt_(f"xd{c}", xd[c][:], q8(4 + 2 * c), mrep(M_XD, 4, c0=0, c1=64), ALU.mult)
                    step(f"svE{c}")
                    dve.tensor_copy(sv[c][64:128, :, 0, :], q8(4 + 2 * c, slice(64, 128), 256)).then_inc(V, 1)
                    step(f"svO{c}")
                    dve.tensor_copy(sv[c][0:64, :, 1, :], q8(4 + 2 * c, slice(0, 64), 256)).then_inc(V, 1)

                def grow(name, st_, bank, first=None):
                    for c in pr.chs:
                        dve.wait_ge(Tn, pr.at("T", f"{st_}{c}"))
                        tt_(f"{name}{c}", pt[c][:], pt[c][:], q8(bank + 2 * c), ALU.add)

                grow("pt2", "s2_", 5)
                grow("pt3", "s3_", 5)
                grow("dt", "s4_", 4)
                grow("rr", "s7_", 5)
                grow("tt", "s8_", 4)
                for c in pr.chs:
                    b0_, b1_ = 4 + 2 * c, 5 + 2 * c
                    dve.wait_ge(Tn, pr.at("T", f"q0{c}"))
                    dve.wait_ge(A, pr.at("A", f"zl{c}"))
                    tt_(f"x{c}", yo[c][:], zl[c][:], q8(b1_), ALU.add)
                    dve.wait_ge(Tn, pr.at("T", f"sa{c}"))
                    step(f"saE{c}")
                    dve.tensor_copy(sv[c][0:64, :, 0, :], q8(b1_, slice(0, 64))).then_inc(V, 1)
                    step(f"saO{c}")
                    dve.tensor_copy(sv[c][64:128, :, 1, :], q8(b1_, slice(64, 128))).then_inc(V, 1)
                    dve.wait_ge(Tn, pr.at("T", f"ds{c}"))
                    tt_(f"st1{c}", st[:], st[:], q8(b1_), ALU.add)
                    own(f"st1{c}")
                    pcv = pcf[:, 0:4 * n].rearrange("p (a c) -> p a c", c=n)[:, :, c:c + 1].to_broadcast([128, 4, CH])
                    tt_(f"st2{c}", st[:], st[:], pcv, ALU.mult)
                    dve.wait_ge(Tn, pr.at("T", f"o2{c}"))
                    o_ = v4(ip)[:, :, CH * c:CH * c + CH]
                    tt_(f"o{c}", o_, o_, q8(b0_), ALU.add)
                dve.wait_ge(Tn, pr.at("T", "mean"))
                tt_("oc", fl(ip), fl(ip), ps(4), ALU.subtract)
                dve.wait_ge(A, pr.at("A", "v2"))
                tt_("on", fl(ip), fl(ip), fl(zz), ALU.mult)
                own("on")
                tt_("lg", v4(ip), v4(ip), cv(C_LG, 4, W), ALU.mult)
                own("lg")
                dve.wait_ge(G, pr.at("G", "lb"))
                tt_("ob", fl(ip), fl(ip), fl(kt), ALU.add)
                own("ob")
                rv = rwp[:, 0:4, 0:W] if pr.sample else rwp[:, 0:4, bass.ds(pr.tok, W)]
                tt_("gate", rv, v4(ip), v4(gg), ALU.mult)
                step("km")
                dve.memset(kmask[:], 0.0).then_inc(V, 1)
                step.end()

            pcf = pcol[:].rearrange("p a c -> p (a c)")

            def body(dve, b, b0):
                T = T_(b0)
                for dest, k, lead_, first in ((rwp, NRW, 1, 0), (q, 4, 0, NRW), (kvp, 2, CH, NRW + 4)):
                    with dve.Fori(0, k // 2) as i:
                        for p in range(2):
                            split(b, first + p + 1, i)
                            dve.wait_ge(mm_done, mmd(ring(b, first + p, i)))
                            settled(dve)
                            dve.tensor_copy(view(dest[:, i * 2 + p, lead_:lead_ + T], b0),
                                            psv(2 * p, b0)).then_inc(bank_free, 1)
                if b0:
                    pair_steps(b, b0, Pair(None, 0), None)
                    dve.wait_ge(s_sstate, 16)
                    dve.memset(st[:], 0.0).then_inc(s_reset, 1)
                    dve.wait_ge(rw["V"], Pair(None, 0).all("V"))
                    dve.memset(kmask[:, 0, 0:CH], NEG).then_inc(s_reset, 1)
                with dve.Fori(0, NPAIR) as i:
                    pair_steps(b, b0, Pair(b * NPAIR + i, i * 128 + (CH if b0 else 0)), i)
                with dve.Fori(0, KD) as d:
                    split(b, U_BR + 1, d)
                    split(b, U_BR + 2, d)
                    dve.wait_ge(gates, b * KD + d + 1)
                    dve.wait_ge(mm_done, mmd(ring(b, U_BR + 1, d)))
                    dve.tensor_tensor(view(e2[:, 0:T], b0), view(e2[:, 0:T], b0), psv(4, b0),
                                      ALU.mult).then_inc(v_own, 1)
                    dve.tensor_tensor(view(e1[:, 0:T], b0), view(e1[:, 0:T], b0), psv(6, b0),
                                      ALU.mult).then_inc(bank_free, 1)
                    dve.wait_ge(v_own, b * KD + d + 1)
                    dve.wait_ge(bank_free, free(ring(b, U_BR + 1, d)))
                    dve.wait_ge(m_lo, b * KD + d + 1)
                    settled(dve)
                    dve.tensor_tensor(acc[:, 0:T], e1[:, 0:T], e2[:, 0:T], ALU.add).then_inc(m_sum, 1)

                def residual(off, i, p):
                    split(b, off + 1, i)
                    dve.wait_ge(mm_done, mmd(ring(b, off, i)))
                    dve.wait_ge(xres_ld, b * 16 + 16)
                    settled(dve)
                    xr = xres[:, i * 2 + p, 0:T]
                    dve.tensor_tensor(view(xr, b0), view(xr, b0), psv(2 * p, b0), ALU.add).then_inc(bank_free, 1)

                clear(acc, n2_sum, (m_lo, b * KD + (KD + 1)))
                with dve.Fori(0, KD // 2) as i:
                    for p in range(2):
                        residual(U_WO + p, i, p)
                        add_sq(T, acc, sq[p], n2_sq, b * (2 * KD) + i * 2 + (p + 1), n2_sum, summed(b * 2, i * 2 + p))
                for d in range(KD):
                    dve.wait_ge(n2_rs, b * 4 + 2)
                    if d >= 2:
                        dve.wait_ge(n2_lo, b * KD + (d - 1))
                    settled(dve)
                    scaled(T, sq[d % 2][:, 0:T], xres[:, d, 0:T], C_N2, d, rs).then_inc(n2_t, 1)
                for s, g in enumerate(GROUPS):
                    with dve.Fori(0, g) as i:
                        f = b * NFF + i + sum(GROUPS[:s])
                        split(b, U_F[s] + 1, i)
                        split(b, U_F[s] + 2, i)
                        dve.wait_ge(mm_done, mmd(ring(b, U_F[s] + 1, i)))
                        dve.wait_ge(bank_free, free(ring(b, U_F[s], i)))
                        dve.wait_ge(f_lo, f + 1)
                        dve.tensor_tensor(view(acc[:, 0:T], b0), view(e1[:, 0:T], b0), psv(2, b0),
                                          ALU.mult).then_inc(bank_free, 1)
                    if s == 1:
                        clear(nsum, n1_sum, (n2_rs, b * 4 + 2))
                    if s == 2:
                        clear(acc, n2_sum, (f_lo, b * NFF + (NFF + 1)))
                    for i in range(KD // 2) if s == 2 else [None]:
                        with ExitStack() as loop:
                            if s != 2:
                                i = loop.enter_context(dve.Fori(0, KD // 2))
                            down(b, b0, T, s, g, i, residual)
                for d in range(KD):
                    dve.wait_ge(n2_rs, b * 4 + 4)
                    scaled(T, xres[:, d, 0:T], xres[:, d, 0:T], C_NF, d, rs).then_inc(y_done, 1)

            def down(b, b0, T, s, g, i, residual):
                for p in range(2):
                    if s == 2:
                        dve.wait_ge(n1_rs, b * 2 + 4)
                        dve.wait_ge(n1_lo, b * KD + (i * 2 + p + KD - 1))
                        settled(dve)
                        scaled(BT, nt[p][:, 0:BT], xin[:, i * 2 + p, 0:BT], C_N1, i * 2 + p, nrs).then_inc(n1_t, 1)
                    residual(U_F[s] + 2 * g + p, i, p)
                    if s == 1:
                        add_sq(BT, nsum, nt[p], n1_sq, b * KD + i * 2 + (p + KD + 1),
                               n1_sum, b * (KD + 1) + i * 2 + (p + KD + 2))
                    if s == 2:
                        add_sq(T, acc, sq[p], n2_sq, b * (2 * KD) + (i * 2 + p + KD + 1),
                               n2_sum, summed(b * 2 + 1, i * 2 + p))

            for c, value in enumerate((RMS_EPS, GN_EPS, 10 * LN2)):
                dve.memset(bias[:, c:c + 1], value).then_inc(ini, 1)
            dve.memset(scanm[:], 1.0).then_inc(ini, 1)
            dve.memset(vmask[:, 0:NSAMP], 1.0).then_inc(ini, 1)
            dve.memset(vmask[:, NSAMP:CH], 0.0).then_inc(m_sum, 1)
            dve.memset(kmask[:], 0.0).then_inc(ini, 1)
            dve.wait_ge(ini, 6)
            dve.memset(scanm[:, :, 0:1], 0.0).then_inc(bank_free, 2)
            dve.memset(kmask[:, 0, CH + NSAMP:128], NEG).then_inc(n2_sum, 1)
            dve.memset(nsum[:], 0.0).then_inc(n1_sum, 1)
            for d in range(KD):
                add_sq(MT, nsum, nt[d % 2], n1_sq, d + 1, n1_sum, d + 1)
            split(0, 0, 0)
            dve.wait_ge(n1_rs, 2)
            for d in range(KD):
                if d >= 2:
                    dve.wait_ge(n1_lo, d - 1)
                scaled(MT, nt[d % 2][:], xin[:, d, :], C_N1, d, nrs).then_inc(n1_t, 1)
            dve.wait_ge(bank_free, 2)
            dve.wait_ge(m_sum, 1)
            dve.wait_ge(n2_sum, 1)
            blocks(dve, body)


def kernel(**inputs):
    import numpy as np
    import concourse.bacc as bacc
    from concourse.bass_utils import run_bass_kernel_spmd

    a = {name: np.asarray(v) for name, v in inputs.items()}
    f32 = np.float32

    def planes(m):
        return m.reshape(m.shape[0], -1, 128).transpose(2, 1, 0)

    x = np.zeros((128, KD, NTOK + BT), f32)
    x[:, :, 0:NSAMP] = planes(a["x_sample"][0])
    x[:, :, CH:NTOK] = planes(a["x_prompt"][0])

    heads = [h for j in range(4) for h in (j, j + 4)]
    q_rows = np.concatenate([np.arange(64 * h, 64 * h + 64) for h in heads])
    w_in, w_branch = a["w_in"][0], a["w_branch"][0]
    gates = w_in[:, (NPL * 128):]
    units = [w_in[:, 128 * j:128 * j + 128] for j in range(6, NPL)]
    units += [w_in[:, q_rows][:, 128 * j:128 * j + 128] for j in range(4)]
    units += [w_in[:, 128 * j:128 * j + 128] for j in range(4, 6)]
    units += [gates[:, 128 * j:128 * j + 128] for j in range(KD)]
    both = np.concatenate([w_branch[0][q_rows], w_branch[1]])
    for d in range(KD):
        c = slice(128 * d, 128 * d + 128)
        units += [gates[:, D:][:, c], both[:, c]]
    units += [a["w_out"][0][:, 128 * j:128 * j + 128] for j in range(KD)]
    first = 0
    for g in GROUPS:
        for j in range(first, first + g):
            c = slice(128 * j, 128 * j + 128)
            units += [a["w_ffn_gate"][0][:, c], a["w_ffn_up"][0][:, c]]
        for j in range(KD):
            part = np.zeros((D, 128), f32)
            part[0:128 * g] = a["w_ffn_down"][0][128 * first:128 * (first + g), 128 * j:128 * j + 128]
            units.append(part)
        first += g
    w = np.stack(units).reshape(NU, KD, 128, 128).transpose(0, 2, 1, 3).reshape(NU, 128, WU)

    def cols(v):
        return v.reshape(-1, 128).T

    sinks = np.repeat(a["attn_sinks"][0].reshape(2, 4), 64, axis=0)
    col = np.concatenate([cols(a[n][0]) for n in ("mu_shift", "w0", "a0", "k_k", "k_a")]
                         + [cols(a["r_k"][0].reshape(-1)), cols(a["lnx_g"][0]), cols(a["lnx_b"][0]),
                            cols(a["norm1_g"][0]), cols(a["norm2_g"][0]), cols(a["final_norm_g"]), sinks], axis=1)

    p, f = np.arange(128)[:, None], np.arange(128)[None, :]
    s, t = p % 64, f % 64
    mats = np.zeros((128, NMAT, 128), f32)
    mats[:, M_ID] = p == f
    mats[:, M_ONE] = 1
    mats[:, M_HEAD] = p // 64 == f // 64
    mats[:, M_MEAN] = (p // 64 == f // 64) / 64.0
    mats[:, M_LM] = np.where(f < 64, s <= t, s < t)
    mats[:, M_YD] = np.where(f < 64, s // 16 == t // 16, s // 16 != t // 16) & (s < t)
    mats[:, M_XD] = np.where(f < 64, (s // 16 == t // 16) & (s > t), s == t)

    loras = np.zeros((128, 2, 512), f32)
    loras[0:64, 0], loras[64:128, 0], loras[:, 1] = a["w2"][0], a["a2"][0], a["g2"][0]

    def kv_in(m):
        return m.reshape(128, 128).T

    arrays = {
        "x": x, "w": w, "col": col, "mats": mats, "loras": loras,
        "kv_cache": np.stack([kv_in(a["cache_attn_k"][0, 0]), kv_in(a["cache_attn_v"][0, 0])], axis=1),
        "st_in": a["state_rwkv"][0, 0].reshape(4, 2, 64, 64).transpose(1, 3, 0, 2).reshape(128, 4, 64),
        "shift_in": a["state_shift"][0, 0].reshape(NRW, 128).T[:, :, None],
    }
    arrays = {n: np.ascontiguousarray(v) for n, v in arrays.items()}
    outs = {"y": (128, KD, NTOK), "st_s": (128, 4, 64), "st_p": (128, 4, 64), "shift_s": (128, NRW, 1),
            "shift_p": (128, NRW, 1), "kv_s": (128, 2, 128), "kv_p": (128, 2, 128)}
    nc = bacc.Bacc("TRN2", target_bir_lowering=False, num_devices=1)
    args = [nc.dram_tensor(n, v.shape, F32, kind="ExternalInput").ap() for n, v in arrays.items()]
    args += [nc.dram_tensor(n, s_, F32, kind="ExternalOutput").ap() for n, s_ in outs.items()]
    hybrid_layer(nc, *args)
    r = run_bass_kernel_spmd(nc, [arrays], core_ids=[0]).results[0]

    y = r["y"].transpose(2, 1, 0).reshape(NTOK, D)

    def kv_out(m, which):
        return m[:, which].T.reshape(1, 1, 128, 2, 64)

    def state_out(m):
        return m.reshape(2, 64, 4, 64).transpose(2, 0, 3, 1).reshape(1, 1, 8, 64, 64)

    def shift_out(m):
        return m[:, :, 0].T.reshape(1, 1, 1, NRW * 128)

    return (y[None, CH:], y[None, 0:NSAMP],
            kv_out(r["kv_p"], 0), kv_out(r["kv_p"], 1), state_out(r["st_p"]), shift_out(r["shift_p"]),
            kv_out(r["kv_s"], 0), kv_out(r["kv_s"], 1), state_out(r["st_s"]), shift_out(r["shift_s"]))
```
